# Optimizing a Trainium2 kernel written in Bass

```python
import jax, jax.numpy as jnp
from jax import lax
import numpy as np

D_MODEL = 1024
BATCH = 1
SEQ = 256
DEPTH = 2

MEM_LEN = 256
HEAD_DIM = 64
POOL_WINDOWS = (2, 4, 8, 16)
POOL_WIDTH = D_MODEL // 4
POOL_GROUP = POOL_WIDTH // len(POOL_WINDOWS)
DSA_HEADS = 8
DSA_WIDTH = DSA_HEADS * HEAD_DIM
DSA_PATTERNS = ((128, 1), (512, 4), (2048, 16))
DSA_BLOCK = 128
MEM_HEADS = 4
MEM_WIDTH = MEM_HEADS * HEAD_DIM
MIX_WIDTH = POOL_WIDTH + DSA_WIDTH + MEM_WIDTH
IN_WIDTH = POOL_WIDTH + 3 * DSA_WIDTH + MEM_WIDTH
SPLITS = (POOL_WIDTH, POOL_WIDTH + DSA_WIDTH, POOL_WIDTH + 2 * DSA_WIDTH, POOL_WIDTH + 3 * DSA_WIDTH)
ROPE_THETA = 500000.0
ROT_DIM = HEAD_DIM // 4
N_EXPERTS = 64
TOP_K = 8
N_GROUPS = 8
TOPK_GROUPS = 4
D_EXPERT = 256
D_SHARED = 256
ROUTED_SCALE = 2.5
MOE_BLOCK = 128
LN_EPS = 1e-5
DEEPNORM_ALPHA = (2 * DEPTH) ** 0.25
DEEPNORM_BETA = (8 * DEPTH) ** -0.25

kernel_name = "hybrid_pool_dilated_mem_moe_deepnorm"

F32 = jnp.float32

def layer_norm(x, g, b):
    xf = x.astype(F32)
    mu = xf.mean(-1, keepdims=True)
    var = jnp.square(xf - mu).mean(-1, keepdims=True)
    return ((xf - mu) * lax.rsqrt(var + LN_EPS) * g.astype(F32) + b.astype(F32)).astype(x.dtype)

def rope_tables(S):
    pos = jnp.arange(S, dtype=F32)
    inv = ROPE_THETA ** (-jnp.arange(0, ROT_DIM, 2, dtype=F32) / ROT_DIM)
    ang = pos[:, None] * inv[None, :]
    return jnp.cos(ang), jnp.sin(ang)

def partial_rotary(x, cos, sin):
    half = ROT_DIM // 2
    xr = x[..., :ROT_DIM].astype(F32)
    x1, x2 = xr[..., :half], xr[..., half:]
    c, s = cos[None, :, None, :], sin[None, :, None, :]
    rot = jnp.concatenate([x1 * c - x2 * s, x2 * c + x1 * s], axis=-1).astype(x.dtype)
    return jnp.concatenate([rot, x[..., ROT_DIM:]], axis=-1)

def multiscale_pool(u, w_pool, pool_scale):
    B, S, _ = u.shape
    grp = u.astype(F32).reshape(B, S, len(POOL_WINDOWS), POOL_GROUP)
    csum = jnp.cumsum(grp, axis=1)
    t = jnp.arange(S)
    outs = []
    for g, w in enumerate(POOL_WINDOWS):
        cg = csum[:, :, g]
        lag = jnp.pad(cg, ((0, 0), (w, 0), (0, 0)))[:, :S]
        cnt = jnp.minimum(t + 1, w).astype(F32)[None, :, None]
        outs.append((cg - lag) / cnt - grp[:, :, g])
    pooled = jnp.stack(outs, axis=2).astype(u.dtype)
    mixed = jnp.einsum('bsgc,gcd->bsgd', pooled, w_pool)
    return mixed.reshape(B, S, POOL_WIDTH) * pool_scale

def dilated_window_branch(q, k, v, dilation, lookback):
    B, S, H, Dh = q.shape
    L = S // dilation
    nb = -(-L // DSA_BLOCK)
    Lp = nb * DSA_BLOCK

    def split(a):
        a = a.reshape(B, L, dilation, H, Dh)
        return jnp.pad(a, ((0, 0), (0, Lp - L), (0, 0), (0, 0), (0, 0)))

    def band(a):
        a = jnp.pad(split(a), ((0, 0), (DSA_BLOCK, 0), (0, 0), (0, 0), (0, 0)))
        a = a.reshape(B, nb + 1, DSA_BLOCK, dilation, H, Dh)
        return jnp.concatenate([a[:, :-1], a[:, 1:]], axis=2)

    qs = split(q).reshape(B, nb, DSA_BLOCK, dilation, H, Dh).astype(F32)
    kb, vb = band(k).astype(F32), band(v).astype(F32)
    s = jnp.einsum('bnqrhd,bnkrhd->bnrhqk', qs, kb) * (Dh ** -0.5)
    qi = jnp.arange(DSA_BLOCK)[:, None]
    kj = jnp.arange(2 * DSA_BLOCK)[None, :]
    diff = qi + DSA_BLOCK - kj
    key_row = (jnp.arange(nb)[:, None, None] - 1) * DSA_BLOCK + kj[None]
    valid = ((diff >= 0) & (diff <= lookback))[None] & (key_row >= 0)
    s = jnp.where(valid[None, :, None, None], s, -jnp.inf)
    m = s.max(-1, keepdims=True)
    p = jnp.exp(s - m)
    den = p.sum(-1, keepdims=True)
    o = jnp.einsum('bnrhqk,bnkrhd->bnqrhd', p / den, vb)
    lse = (m + jnp.log(den))[..., 0]
    o = o.reshape(B, Lp, dilation, H, Dh)[:, :L].reshape(B, S, H, Dh)
    lse = lse.transpose(0, 1, 4, 2, 3).reshape(B, Lp, dilation, H)[:, :L].reshape(B, S, H)
    return o, lse

def dilated_attention(q, k, v):
    outs, lses = [], []
    for window, dilation in DSA_PATTERNS:
        o, lse = dilated_window_branch(q, k, v, dilation, window // dilation)
        outs.append(o)
        lses.append(lse)
    wts = jax.nn.softmax(jnp.stack(lses, axis=0), axis=0)
    return jnp.einsum('pbsh,pbshd->bshd', wts, jnp.stack(outs, axis=0))

def memory_attention(q, k, v):
    s = jnp.einsum('bshd,bmhd->bhsm', q.astype(F32), k.astype(F32)) * (HEAD_DIM ** -0.5)
    p = jax.nn.softmax(s, axis=-1)
    return jnp.einsum('bhsm,bmhd->bshd', p, v.astype(F32))

def hybrid_mixer(x, mem, w_in, w_pool, pool_scale, w_mem_kv, w_out, cos, sin):
    B, S, _ = x.shape
    h = x @ w_in
    u, q, k, v, qm = jnp.split(h, list(SPLITS), axis=-1)
    heads = lambda a: a.reshape(a.shape[0], a.shape[1], -1, HEAD_DIM)
    q = partial_rotary(heads(q), cos, sin)
    k = partial_rotary(heads(k), cos, sin)
    y_pool = multiscale_pool(u, w_pool, pool_scale)
    y_dsa = dilated_attention(q, k, heads(v)).astype(x.dtype).reshape(B, S, DSA_WIDTH)
    km, vm = jnp.split(mem @ w_mem_kv, 2, axis=-1)
    y_mem = memory_attention(heads(qm), heads(km), heads(vm)).astype(x.dtype).reshape(B, S, MEM_WIDTH)
    return jnp.concatenate([y_pool, y_dsa, y_mem], axis=-1) @ w_out

def swiglu(x, wg, wu, wd):
    return (jax.nn.silu(x @ wg) * (x @ wu)) @ wd

def route(xf, w_router, router_bias):
    N = xf.shape[0]
    scores = jax.nn.sigmoid((xf @ w_router).astype(F32))
    biased = scores + router_bias.astype(F32)
    grp_score = lax.top_k(biased.reshape(N, N_GROUPS, -1), 2)[0].sum(-1)
    _, grp_idx = lax.top_k(grp_score, TOPK_GROUPS)
    grp_mask = jax.nn.one_hot(grp_idx, N_GROUPS, dtype=F32).sum(-2) > 0
    expert_mask = jnp.repeat(grp_mask, N_EXPERTS // N_GROUPS, axis=-1)
    _, top_idx = lax.top_k(jnp.where(expert_mask, biased, -jnp.inf), TOP_K)
    top_w = jnp.take_along_axis(scores, top_idx, axis=-1)
    top_w = top_w / top_w.sum(-1, keepdims=True) * ROUTED_SCALE
    return top_idx, top_w

def routed_experts(xf, top_idx, top_w, w_gate, w_up, w_down):
    N, D = xf.shape
    A = N * TOP_K
    e_flat = top_idx.reshape(A)
    tok_flat = jnp.repeat(jnp.arange(N, dtype=jnp.int32), TOP_K)
    order = jnp.argsort(e_flat)
    e_sorted, tok_sorted = e_flat[order], tok_flat[order]
    w_sorted = top_w.reshape(A)[order]
    counts = jnp.bincount(e_flat, length=N_EXPERTS)
    padded = (counts + MOE_BLOCK - 1) // MOE_BLOCK * MOE_BLOCK
    pend = jnp.cumsum(padded)
    pstart = pend - padded
    start = jnp.cumsum(counts) - counts
    dest = pstart[e_sorted] + jnp.arange(A) - start[e_sorted]
    n_blocks = -(-A // MOE_BLOCK) + N_EXPERTS
    rows_tok = jnp.zeros((n_blocks * MOE_BLOCK,), jnp.int32).at[dest].set(tok_sorted)
    block_e = jnp.minimum(jnp.searchsorted(pend, jnp.arange(n_blocks) * MOE_BLOCK, side='right'), N_EXPERTS - 1)
    xb = xf[rows_tok].reshape(n_blocks, MOE_BLOCK, D)

    def expert_block(args):
        xblk, e = args
        return swiglu(xblk, w_gate[e], w_up[e], w_down[e])

    yb = lax.map(expert_block, (xb, block_e)).reshape(n_blocks * MOE_BLOCK, D)
    contrib = yb[dest] * w_sorted[:, None].astype(yb.dtype)
    return jax.ops.segment_sum(contrib, tok_sorted, num_segments=N)

def moe_ffn(x, w_router, router_bias, w_gate, w_up, w_down, ws_gate, ws_up, ws_down):
    B, S, D = x.shape
    xf = x.reshape(B * S, D)
    top_idx, top_w = route(xf, w_router, router_bias)
    y = routed_experts(xf, top_idx, top_w, w_gate, w_up, w_down) + swiglu(xf, ws_gate, ws_up, ws_down)
    return y.reshape(B, S, D)

def setup_inputs(seed: int = 0) -> dict:
    key = jax.random.key(seed)
    ks = jax.random.split(key, 20)
    nrm = lambda k, shape, scale: jax.random.normal(k, shape, F32) * scale
    L, D, E = DEPTH, D_MODEL, N_EXPERTS
    return {
        "x": nrm(ks[0], (BATCH, SEQ, D), 1.0),
        "mem": nrm(ks[1], (BATCH, MEM_LEN, D), 1.0),
        "w_in": nrm(ks[2], (L, D, IN_WIDTH), D ** -0.5),
        "w_pool": nrm(ks[3], (L, len(POOL_WINDOWS), POOL_GROUP, POOL_GROUP), POOL_GROUP ** -0.5),
        "pool_scale": 1.0 + nrm(ks[4], (L, POOL_WIDTH), 0.1),
        "w_mem_kv": nrm(ks[5], (L, D, 2 * MEM_WIDTH), D ** -0.5),
        "w_out": nrm(ks[6], (L, MIX_WIDTH, D), MIX_WIDTH ** -0.5 * DEEPNORM_BETA),
        "ln1_g": 1.0 + nrm(ks[7], (L, D), 0.02),
        "ln1_b": nrm(ks[8], (L, D), 0.02),
        "w_router": nrm(ks[9], (L, D, E), D ** -0.5),
        "router_bias": nrm(ks[10], (L, E), 0.01),
        "w_gate": nrm(ks[11], (L, E, D, D_EXPERT), D ** -0.5),
        "w_up": nrm(ks[12], (L, E, D, D_EXPERT), D ** -0.5),
        "w_down": nrm(ks[13], (L, E, D_EXPERT, D), D_EXPERT ** -0.5 * DEEPNORM_BETA),
        "ws_gate": nrm(ks[14], (L, D, D_SHARED), D ** -0.5),
        "ws_up": nrm(ks[15], (L, D, D_SHARED), D ** -0.5),
        "ws_down": nrm(ks[16], (L, D_SHARED, D), D_SHARED ** -0.5 * DEEPNORM_BETA),
        "ln2_g": 1.0 + nrm(ks[17], (L, D), 0.02),
        "ln2_b": nrm(ks[18], (L, D), 0.02),
    }

def reference(x, mem, w_in, w_pool, pool_scale, w_mem_kv, w_out, ln1_g, ln1_b, w_router, router_bias,
              w_gate, w_up, w_down, ws_gate, ws_up, ws_down, ln2_g, ln2_b):
    cos, sin = rope_tables(x.shape[1])
    for l in range(DEPTH):
        mix = hybrid_mixer(x, mem, w_in[l], w_pool[l], pool_scale[l], w_mem_kv[l], w_out[l], cos, sin)
        x = layer_norm(DEEPNORM_ALPHA * x + mix, ln1_g[l], ln1_b[l])
        ffn = moe_ffn(x, w_router[l], router_bias[l], w_gate[l], w_up[l], w_down[l],
                      ws_gate[l], ws_up[l], ws_down[l])
        x = layer_norm(DEEPNORM_ALPHA * x + ffn, ln2_g[l], ln2_b[l])
    return x


_drawn_inputs = setup_inputs


def setup_inputs(seed=0):
    import zlib

    import numpy as np

    out = dict(_drawn_inputs(seed))
    spreads = {}
    factors = {}
    for name, (base, spread) in spreads.items():
        noise = np.random.default_rng([zlib.crc32(name.encode()), seed]).standard_normal(out[name].shape)
        drawn = base * np.exp(spread * noise) if base else spread * noise
        out[name] = __import__('jax').numpy.asarray(drawn.astype(out[name].dtype))
    for name, factor in factors.items():
        out[name] = (out[name] * factor).astype(out[name].dtype)
    return out
```

```python
from contextlib import ExitStack

import numpy as np
import concourse.bass as bass
from concourse import mybir

F32 = mybir.dt.float32
BF16 = mybir.dt.bfloat16
I32 = mybir.dt.int32
ALU = mybir.AluOpType
ACT = mybir.ActivationFunctionType
AX = mybir.AxisListType

P = 128
DEPTH, D, S = 2, 1024, 256
NT = S // P
KD = D // P
HD = 64
DSA_HEADS, MEM_HEADS = 8, 4
SCALE = HD ** -0.5
WINDOWS = (2, 4, 8, 16)
PATTERNS = ((128, 1), (512, 4), (2048, 16))
ROT = HD // 4
POOL_W = D // 4
E, TOPK, GROUPS, TOP_GROUPS = 64, 8, 8, 4
F = 256
KF = F // P
SLOTS = 64
PAIRS = E // 2
ROUNDS = S // SLOTS
ROUTED_SCALE = 2.5
ALPHA = float((2 * DEPTH) ** 0.25)
EPS = 1e-5
BIG = 1e30
GONE = -3e38

CONSTS = {}
_at = 0
for _n, _w in (("ident", P), ("rot", P), ("before", P), ("slot", SLOTS), ("tri", GROUPS * GROUPS),
               ("cos", S), ("sin", S), ("bias", 3 * P), ("mult", 3 * P)):
    CONSTS[_n] = (_at, _at + _w)
    _at += _w
NCONST = _at


def constants():
    c = np.zeros((P, NCONST), np.float32)

    def put(name, v):
        c[:, CONSTS[name][0]:CONSTS[name][1]] = v
    i, j = np.arange(P)[:, None], np.arange(P)[None]
    put("ident", i == j)
    put("before", i < j)
    put("slot", np.arange(SLOTS)[None])
    g = np.arange(GROUPS)
    put("tri", (g[None, :] < g[:, None]).reshape(1, -1))
    half = ROT // 2
    r = np.zeros((P, P))
    for h in range(0, P, HD):
        for d in range(half):
            r[h + d + half, h + d] = -1
            r[h + d, h + d + half] = 1
    put("rot", r)
    inv = np.float32(500000.0) ** (-np.arange(0, ROT, 2, dtype=np.float32) / np.float32(ROT))
    ang = np.arange(S, dtype=np.float32)[:, None] * inv[None]
    cos, sin = np.ones((P, S)), np.zeros((P, S))
    for h in range(0, P, HD):
        for d in range(ROT):
            cos[h + d] = np.cos(ang[:, d % half])
            sin[h + d] = np.sin(ang[:, d % half])
    put("cos", cos)
    put("sin", sin)
    qi, kj = np.arange(S)[:, None], np.arange(S)[None]
    m = np.zeros((S, S))
    for window, dil in PATTERNS:
        d = qi - kj
        m += (d >= 0) & (d % dil == 0) & (d // dil <= window // dil)
    m = np.concatenate([m[:P, :P], m[P:]], axis=1)
    put("mult", m)
    put("bias", np.where(m > 0, 0.0, -BIG))
    s = np.arange(S)
    pool = np.zeros((S, len(WINDOWS), S), np.float32)
    for n, w in enumerate(WINDOWS):
        inside = (qi <= s[None]) & (qi > s[None] - w)
        pool[:, n] = inside / np.minimum(s + 1, w)[None] - (qi == s[None])
    pool = pool.reshape(NT, P, -1).transpose(1, 0, 2).reshape(P, -1)
    return c, np.ascontiguousarray(pool.astype(np.float32))


FILLS = ([(f"xTa{g}", g) for g in range(4)] + [(f"memT{g}", 4 + g) for g in range(4)]
         + [("kmT", 0), ("vm", 1)]
         + [(f"{a}{i}", (2 if a == "raw" else 4) + i % 2) for i in range(4) for a in ("raw", "rot")]
         + [("v0", 6), ("v1", 7), ("u", 0), ("qm", 1), ("pooled", 2), ("pmix", 3)])
UNITS = DSA_HEADS + MEM_HEADS
for _u in range(UNITS):
    FILLS += [(f"s{_u}", 4 + _u % 2)]
    FILLS += [(f"pT{_u}", 6 + _u % 2)]
    if _u % 2:
        FILLS += [(f"o{_u // 2}", (_u // 2) % 2)]
FILLS += [(f"wo{i}", 2 + i) for i in range(4)]
FILLS += [(f"xTb{g}", (6, 7, 0, 1)[g]) for g in range(4)]
FILLS += [("logit", 2), ("cum", 3), ("sh0", 4), ("sh1", 5), ("shT", 6)]
FILLS += [(f"acc{i}", i) for i in range(4)]
PER_BANK = [sum(b == n for _, b in FILLS) for n in range(8)]
BANK_OF = dict(FILLS)
ORDER = {name: sum(b == bank for _, b in FILLS[:i]) for i, (name, bank) in enumerate(FILLS)}

CHUNKS = ["kv", "q", "k", "v", "u", "qm", "wo0", "wo1", "sgu", "sd"]
LAST_USE = ["vm", "raw1", "raw3", "v1", "u", "qm", "wo1", "wo3", "sh1", "acc3"]
NCH = len(CHUNKS)
DVE_LINKS = 59


def build(nc, x, mem, w_in, w_pool, pool_scale, w_mem_kv, w_out, ln1_g, ln1_b, w_router,
          router_bias, w_gate, w_up, w_down, ws_gate, ws_up, ws_down, ln2_g, ln2_b,
          consts, pool_mat, out):
    with ExitStack() as ctx:
        def sb(name, shape, dt=F32):
            return ctx.enter_context(nc.sbuf_tensor(name, shape, dt))

        def sem(name):
            return ctx.enter_context(nc.semaphore(name))

        bank = [ctx.enter_context(nc.psum_tensor(f"bank{i}", [P, 512], F32)) for i in range(8)]
        acc = bank[0:4]
        G, H, Y = bank[4], bank[5], bank[6:8]

        gu = sb("gu", [P, 2, 2, 2, KD, F])
        dn = sb("dn", [P, 2, 2, KF, D])
        stage = sb("stage", [P, 2, KD * 512])
        xs = sb("xs", [P, NT, D])
        xT = sb("xT", [P, KD, S])
        cst = sb("cst", [P, NCONST])
        r8 = sb("r8", [P, 2048])
        small = sb("small", [P, 64])
        identb = sb("identb", [P, P], BF16)
        beforeb = sb("beforeb", [P, P], BF16)
        onesb = sb("onesb", [P, P], BF16)
        wr = sb("wr", [P, KD, E])
        rb = sb("rb", [P, E])
        wp = sb("wp", [P, 2, HD])
        psc = sb("psc", [P, 2])
        epst = sb("epst", [P, 1])
        scratch = sb("scratch", [P, 10752])
        off = [0]

        def part(n, dt=F32):
            v = scratch[:, off[0]:off[0] + n]
            off[0] += n
            assert off[0] <= 10752, off[0]
            return v if dt == F32 else v.bitcast(dt)
        qkT = part(8 * S).rearrange("p (c s) -> p c s", s=S)
        vv = part(NT * 512).rearrange("p (t n) -> p t n", t=NT)
        qmT = part(2 * S).rearrange("p (c s) -> p c s", s=S)
        kmT = part(2 * S).rearrange("p (c s) -> p c s", s=S)
        vm = part(2 * S).rearrange("p (t n) -> p t n", t=2)
        mixT = part(KD * S).rearrange("p (c s) -> p c s", s=S)
        uu = part(NT * 256).rearrange("p (t n) -> p t n", t=NT)
        pooledT = part(2 * S).rearrange("p (c s) -> p c s", s=S)
        raw = part(2 * 512).rearrange("p (b n) -> p b n", b=2)
        rt = part(512)
        pT = part(2 * 512).rearrange("p (b n) -> p b n", b=2)
        memT = mixT
        off[0] = 0
        xsp = part(NT * 3 * D // 2, BF16).rearrange("p (t s d) -> p t s d", t=NT, s=3)
        xres = part(NT * D).rearrange("p (t d) -> p t d", t=NT)
        ysp = part(3 * D // 2, BF16).rearrange("p (s d) -> p s d", s=3)
        xg = part(KD * P).rearrange("p (k c) -> p k c", k=KD)
        hh = part(2 * F).rearrange("p (t n) -> p t n", t=NT)
        hT = part(2 * F)
        sg = part(2 * F).rearrange("p (t n) -> p t n", t=NT)
        sel = part(NT * P // 2, BF16).rearrange("p (t c) -> p t c", t=NT)
        selT = part(2 * S // 2, BF16).rearrange("p (b s) -> p b s", b=2)
        pos = part(NT * E)
        w3 = part(NT * E * 3 // 2, BF16).rearrange("p (t e s) -> p t e s", t=NT, s=3)
        off[0] = NT * 3 * D // 2 + NT * D
        sig = part(NT * E)
        biased = part(NT * E)
        masked = part(NT * E)
        chosen = part(NT * E)
        wts = part(NT * E)
        wres = part(NT * E)
        chosenb = part(NT * E // 2, BF16)
        g8 = part(NT * GROUPS * 8)
        gs = part(NT * GROUPS)
        cmp1 = part(GROUPS * GROUPS)
        cmp2 = part(GROUPS * GROUPS)
        rank = part(NT * GROUPS)
        gneg = part(NT * GROUPS)
        top = part(NT * 8)
        assert off[0] <= NT * 3 * D // 2 + NT * D + 3 * D // 2
        counts_i = sb("counts_i", [P, 1], I32)
        yres = xres[:, 0, :]

        def cc(name):
            return cst[:, CONSTS[name][0]:CONSTS[name][1]]
        ident = cc("ident")
        mem_sb = r8[:].rearrange("p (t d) -> p t d", t=2)
        pool_sb = r8[:].rearrange("p (t g s) -> p t g s", t=NT, g=len(WINDOWS))
        prob = r8[:, 0:1024].rearrange("p (b n) -> p b n", b=2)
        lng, lnb = r8[:, 0:D], r8[:, D:2 * D]

        mx = [small[:, 0:2], small[:, 2:4]]
        negm = [small[:, 4:6], small[:, 6:8]]
        den = [small[:, 8:10], small[:, 10:12]]
        rden = [small[:, 12:14], small[:, 14:16]]
        mv = small[:, 16:20].rearrange("p (t n) -> p t n", t=NT)
        std = small[:, 20:22]
        rstd = small[:, 22:24]
        stats = small[:, 24:48].rearrange("p (t h n) -> p t h n", t=NT, h=2)
        wsum = small[:, 48:50]
        wrec = small[:, 50:52]
        wslot = small[:, 52:54]
        cntf = small[:, 54:55]

        full = [sem(f"bank{i}_full") for i in range(8)]
        read = [sem(f"bank{i}_read") for i in range(8)]
        const_in = sem("const_in")
        carried = sem("carried")
        x_in = sem("x_in")
        setup_done = sem("setup_done")
        mem_in = sem("mem_in")
        small_in = sem("small_in")
        pool_in = sem("pool_in")
        ln_in = sem("ln_in")
        chunk_in = [sem(f"chunk_in{i}") for i in range(2)]
        x_ready = sem("x_ready")
        qk_sb = sem("qk_sb")
        negm_rd = sem("negm_rd")
        exp_rd = sem("exp_rd")
        p_rd = sem("p_rd")
        var_rd = sem("var_rd")
        std_rd = sem("std_rd")
        chosen_rd = sem("chosen_rd")
        route_rd = sem("route_rd")
        split_hi = sem("split_hi")
        split_rs = sem("split_rs")
        split_rd = sem("split_rd")
        ssilu = sem("ssilu")
        pos_rd = sem("pos_rd")
        dve_link = sem("dve_link")
        out_done = sem("out_done")

        class Pass:

            def __init__(self, tag, per_layer):
                self.per_layer = per_layer
                self.sel_rd = sem(f"{tag}_sel_rd")
                self.g_full = sem(f"{tag}_g_full")
                self.g_sb = sem(f"{tag}_g_sb")
                self.selT_ps = sem(f"{tag}_selT_ps")
                self.selT_sb = sem(f"{tag}_selT_sb")
                self.h_full = sem(f"{tag}_h_full")
                self.silu_rd = sem(f"{tag}_silu_rd")
                self.h_rd = sem(f"{tag}_h_rd")
                self.hT_ps = sem(f"{tag}_hT_ps")
                self.hT_sb = sem(f"{tag}_hT_sb")
                self.y_full = sem(f"{tag}_y_full")
                self.hi_rd = sem(f"{tag}_hi_rd")
                self.res_rd = sem(f"{tag}_res_rd")
                self.mid_rd = sem(f"{tag}_mid_rd")
                self.lo_rd = sem(f"{tag}_lo_rd")
                self.comb = sem(f"{tag}_comb")
        main = Pass("main", PAIRS)
        more = Pass("more", PAIRS * (ROUNDS - 1))
        gu_in = [sem(f"gu_in{b}") for b in range(2)]
        dn_in = [sem(f"dn_in{b}") for b in range(2)]
        mgu_in = [sem(f"mgu_in{b}") for b in range(2)]
        mdn_in = [sem(f"mdn_in{b}") for b in range(2)]
        main.w_in = (gu_in, dn_in)
        more.w_in = (mgu_in, mdn_in)

        block = ctx.enter_context(nc.Block())

        def stand_alone(eng):
            eng.sem_inc(carried, 1)

        def full_at(l, name):
            b = BANK_OF[name]
            return full[b], l * PER_BANK[b] + ORDER[name] + 1

        def read_at(l, name):
            b = BANK_OF[name]
            return read[b], l * PER_BANK[b] + ORDER[name] + 2

        def free_at(l, name):
            b = BANK_OF[name]
            return read[b], l * PER_BANK[b] + ORDER[name] + 1

        def pairs_of_pass(eng, base, body):
            for b in range(2):
                body(base + b, b, b, b == 0, False)
            with eng.Fori(1, PAIRS // 2 - 1) as i:
                for b in range(2):
                    body(base + 2 * i + b, 2 * i + b, b, False, False)
            for b in range(2):
                q = PAIRS - 2 + b
                body(base + q, q, b, False, b == 1)

        def passes(eng, l, run, skipped):
            run(main, l * PAIRS, None)
            eng.wait_ge(route_rd, l + 1)
            stand_alone(eng)
            cnt = eng.value_load(counts_i[0:1, 0:1], min_val=0, max_val=S)
            with eng.If(cnt > SLOTS):
                with eng.Fori(0, ROUNDS - 1) as r:
                    run(more, l * more.per_layer + r * PAIRS, l * (ROUNDS - 1) + r)
                eng.nop()
            with eng.Else():
                skipped(more.per_layer)
                eng.nop()

        @block.sync
        def _(sp):
            sp.dma_start(xs[:], x[0].rearrange("(t p) d -> p t d", p=P)).then_inc(x_in, 16)
            sp.dma_start(cst[:], consts).then_inc(const_in, 16)
            kvv = w_mem_kv.rearrange("l (p k) n -> l p k n", k=KD)
            win = w_in.rearrange("l (p k) n -> l p k n", k=KD)
            wov = w_out.rearrange("l (k p) n -> l p k n", p=P)
            sgv = ws_gate.rearrange("l (p k) n -> l p k n", k=KD)
            suv = ws_up.rearrange("l (p k) n -> l p k n", k=KD)
            sdv = ws_down.rearrange("l (p k) n -> l p k n", k=KF)
            gv = w_gate.rearrange("l (r e) (p k) n -> (l r) p e (k n)", e=2, k=KD)
            uv = w_up.rearrange("l (r e) (p k) n -> (l r) p e (k n)", e=2, k=KD)
            dv = w_down.rearrange("l (r e) (p k) n -> (l r) p e (k n)", e=2, k=KF)

            def chunk(l, c):
                half = c % 2
                if c >= 2:
                    sp.wait_ge(*full_at(l, LAST_USE[c - 2]))
                dst = stage[:, half, :].rearrange("p (k n) -> p k n", k=KD)
                name = CHUNKS[c]
                stand_alone(sp)
                s_in = chunk_in[half]
                if name == "sgu":
                    sp.dma_start(dst[:, :, 0:256], sgv[l]).then_inc(s_in, 16)
                    sp.dma_start(dst[:, :, 256:512], suv[l]).then_inc(s_in, 16)
                else:
                    if name == "kv":
                        src = kvv[l]
                    elif name in ("q", "k", "v"):
                        at = POOL_W + 512 * "qkv".index(name)
                        src = win[l][:, :, at:at + 512]
                    elif name in ("u", "qm"):
                        at = 0 if name == "u" else POOL_W + 3 * 512
                        src, dst = win[l][:, :, at:at + 256], dst[:, :, 0:256]
                    elif name in ("wo0", "wo1"):
                        at = 512 * int(name[2])
                        src = wov[l][:, :, at:at + 512]
                    else:
                        src, dst = sdv[l], stage[:, half, 0:KF * D].rearrange("p (k n) -> p k n", k=KF)
                    cut = src.shape[1] // 2
                    sp.dma_start(dst[:, 0:cut], src[:, 0:cut]).then_inc(s_in, 16)
                    sp.dma_start(dst[:, cut:], src[:, cut:]).then_inc(s_in, 16)

            def pair(ps, l, n, q, b, first, at_start):
                if not at_start:
                    sp.wait_ge(ps.h_full, n - 1)
                r = l * PAIRS + q
                gu_s, dn_s = ps.w_in
                sp.dma_start(gu[:, b, :, 0, :, :].rearrange("p e k n -> p e (k n)"), gv[r]).then_inc(gu_s[b], 16)
                sp.dma_start(gu[:, b, :, 1, :, :].rearrange("p e k n -> p e (k n)"), uv[r]).then_inc(gu_s[b], 16)
                if not at_start:
                    sp.wait_ge(ps.y_full, 2 * n - 2)
                sp.dma_start(dn[:, b].rearrange("p e k n -> p e (k n)"), dv[r]).then_inc(dn_s[b], 16)

            with sp.Fori(0, DEPTH) as l:
                sp.wait_ge(x_ready, 2 * l + 1)
                sp.dma_start(mem_sb, mem[0].rearrange("(t p) d -> p t d", p=P)).then_inc(mem_in, 16)
                chunk(l, 0)
                chunk(l, 1)
                sp.dma_start(wr[:], w_router.rearrange("l (p k) e -> l p k e", k=KD)[l]).then_inc(small_in, 16)
                sp.dma_start(rb[:], router_bias.rearrange("l (o e) -> l o e", o=1)[l].to_broadcast([P, E])).then_inc(small_in, 16)
                for g2 in range(2):
                    sp.dma_start(wp[64 * g2:64 * g2 + 64], w_pool.rearrange("l (j h) c d -> l h c j d", h=2)[l, g2]).then_inc(small_in, 16)
                sp.dma_start(psc[:], pool_scale.rearrange("l (j p) -> l p j", p=P)[l], allow_slow_non_contiguous=True).then_inc(small_in, 16)
                for c in range(2, 4):
                    chunk(l, c)
                for g in range(4):
                    sp.wait_ge(*full_at(l, f"memT{g}"))
                sp.dma_start(r8[:], pool_mat).then_inc(pool_in, 16)
                chunk(l, 4)
                pair(main, l, None, 0, 0, True, True)
                chunk(l, 5)
                chunk(l, 6)
                pair(main, l, None, 1, 1, True, True)
                chunk(l, 7)
                sp.wait_ge(*full_at(l, f"pT{UNITS - 1}"))
                sp.dma_start(lng, ln1_g.rearrange("l (o d) -> l o d", o=1)[l].to_broadcast([P, D])).then_inc(ln_in, 16)
                sp.dma_start(lnb, ln1_b.rearrange("l (o d) -> l o d", o=1)[l].to_broadcast([P, D])).then_inc(ln_in, 16)
                chunk(l, 8)
                chunk(l, 9)
                sp.wait_ge(x_ready, 2 * l + 2)
                sp.dma_start(lng, ln2_g.rearrange("l (o d) -> l o d", o=1)[l].to_broadcast([P, D])).then_inc(ln_in, 16)
                sp.dma_start(lnb, ln2_b.rearrange("l (o d) -> l o d", o=1)[l].to_broadcast([P, D])).then_inc(ln_in, 16)

                def run(ps, base, round_):
                    if round_ is not None:
                        for b in range(2):
                            pair(ps, l, None, b, b, True, True)
                    with sp.Fori(1, PAIRS // 2) as i:
                        for b in range(2):
                            pair(ps, l, base + 2 * i + b, 2 * i + b, b, False, False)
                    sp.wait_ge(ps.comb, base + PAIRS)
                    stand_alone(sp)

                def skipped(n):
                    for s_, k in ((mgu_in, 16), (mdn_in, 8)):
                        for b in range(2):
                            sp.sem_inc(s_[b], n * k)
                passes(sp, l, run, skipped)
            sp.wait_ge(x_ready, 2 * DEPTH + 1)
            sp.dma_start(out[0].rearrange("(t p) d -> p t d", p=P), xs[:]).then_inc(out_done, 16)
            sp.wait_ge(out_done, 16)

        @block.tensor
        def _(pe):
            pe.wait_ge(const_in, 16)
            pe.wait_ge(x_in, 16)
            pe.wait_ge(setup_done, 1)

            def fill(l, name):
                pe.wait_ge(*free_at(l, name))
                return bank[BANK_OF[name]]

            def filled(l, name, ins):
                ins.then_inc(full[BANK_OF[name]], 1)

            def chunk_wait(l, c):
                pe.wait_ge(chunk_in[c % 2], l * (32 * NCH // 2) + 32 * (c // 2 + 1))

            def transposes(l, tag, src):
                for g in range(4):
                    o = fill(l, f"{tag}{g}")
                    for kk in range(2):
                        for t in range(NT):
                            k = 2 * g + kk
                            m = pe.transpose(o[:, kk * S + t * P:kk * S + t * P + P], src[:, t, k::KD], ident)
                    filled(l, f"{tag}{g}", m)

            def gather(ps, n, half, g_free):
                for w in g_free:
                    pe.wait_ge(*w)
                for kk in range(4):
                    k = 4 * half + kk
                    for j in range(3 * NT):
                        t, s = j // 3, j % 3
                        m = pe.matmul(G[:, kk * P:(kk + 1) * P], xsp[:, t, s, k::KD], sel[:, t, :],
                                      start=j == 0, stop=j == 3 * NT - 1)
                m.then_inc(ps.g_full, 1)

            def turn_sel(ps, n, q):
                pe.wait_ge(ps.g_sb, 2 * n + 2)
                gb = G[:].bitcast(BF16)
                for t in range(NT):
                    pe.transpose(gb[:, t * P:(t + 1) * P], sel[:, t, :], identb[:])
                for t in range(NT):
                    wq = w3[:, t].rearrange("p (r e) s -> p r (e s)", e=2)
                    m = pe.matmul(G[:, 256:262], sel[:, t, :], wq[:, q, :],
                                  start=t == 0, stop=t == NT - 1)
                m.then_inc(ps.selT_ps, 1)

            def combine(ps, n, b):
                pe.wait_ge(ps.lo_rd, 2 * n + 2)
                for t in range(NT):
                    for half in range(2):
                        for s in range(3):
                            m = pe.matmul(acc[2 * t + half][:, :], selT[:, b, t * P:(t + 1) * P],
                                          ysp[:, s, half * 512:(half + 1) * 512],
                                          start=False, stop=False, skip_group_check=True)
                m.then_inc(ps.comb, 1)

            def run(ps, base, round_):
                n0 = base
                pe.wait_ge(ps.sel_rd, n0 + 1)
                gather(ps, n0, 0, [])
                gather(ps, n0, 1, [(ps.g_sb, 2 * n0 + 1)])
                turn_sel(ps, n0, 0)

                def body(n, q, b, first, last):
                    pe.wait_ge(ps.g_sb, 2 * n + 2)
                    pe.wait_ge(ps.w_in[0][b], (n - b) * 16 + 32)
                    if not first:
                        pe.wait_ge(ps.hT_sb, n)
                    for k in range(KD):
                        for a in range(2):
                            m = pe.matmul(H[64 * a:64 * a + 64, :], xg[:, k, 64 * a:64 * a + 64],
                                          gu[:, b, a, :, k, :], start=k == 0, stop=k == KD - 1)
                    m.then_inc(ps.h_full, 1)
                    if not last:
                        pe.wait_ge(ps.sel_rd, n + 2)
                        gather(ps, n + 1, 0, [(ps.selT_sb, n + 1)])
                    if not first:
                        combine(ps, n - 1, 1 - b)
                    pe.wait_ge(ps.h_rd, n + 1)
                    for kc in range(KF):
                        m = pe.transpose(H[:, kc * P:(kc + 1) * P], hh[:, 0, kc::KF], ident)
                    m.then_inc(ps.hT_ps, 1)
                    if not last:
                        gather(ps, n + 1, 1, [(ps.g_sb, 2 * n + 3)])
                    pe.wait_ge(ps.w_in[1][b], (n - b) * 8 + 16)
                    pe.wait_ge(ps.hT_sb, n + 1)
                    for half in range(2):
                        if not first:
                            pe.wait_ge(ps.res_rd, 2 * n - 1 + half)
                        for kc in range(KF):
                            for a in range(2):
                                m = pe.matmul(Y[half][64 * a:64 * a + 64, :],
                                              hT[:, kc * P + 64 * a:kc * P + 64 * a + 64],
                                              dn[:, b, a, kc, half * 512:(half + 1) * 512],
                                              start=kc == 0, stop=kc == KF - 1)
                        m.then_inc(ps.y_full, 1)
                    if not last:
                        turn_sel(ps, n + 1, q + 1)
                pairs_of_pass(pe, base, body)
                combine(ps, base + PAIRS - 1, 1)

            def skipped(n):
                for s_, k in ((more.g_full, 2), (more.selT_ps, 1), (more.h_full, 1), (more.hT_ps, 1),
                              (more.y_full, 2), (more.comb, 1)):
                    pe.sem_inc(s_, n * k)

            with pe.Fori(0, DEPTH) as l:
                pe.wait_ge(x_ready, 2 * l + 1)
                transposes(l, "xTa", xs)
                pe.wait_ge(mem_in, 16 * l + 16)
                transposes(l, "memT", mem_sb)
                chunk_wait(l, 0)
                for g in range(4):
                    pe.wait_ge(*read_at(l, f"memT{g}"))
                W = [stage[:, h, :].rearrange("p (k n) -> p k n", k=KD) for h in range(2)]
                o = fill(l, "kmT")
                for j in range(2):
                    for k in range(KD):
                        m = pe.matmul(o[:, j * S:(j + 1) * S], W[0][:, k, j * P:(j + 1) * P], memT[:, k, :],
                                      start=k == 0, stop=k == KD - 1)
                filled(l, "kmT", m)
                o = fill(l, "vm")
                for t in range(2):
                    for k in range(KD):
                        m = pe.matmul(o[:, t * 256:(t + 1) * 256], memT[:, k, t * P:(t + 1) * P], W[0][:, k, 256:512],
                                      start=k == 0, stop=k == KD - 1)
                filled(l, "vm", m)
                for g in range(4):
                    pe.wait_ge(*read_at(l, f"xTa{g}"))

                def rotate(i):
                    o = fill(l, f"rot{i}")
                    pe.wait_ge(*read_at(l, f"raw{i}"))
                    filled(l, f"rot{i}", pe.matmul(o[:, :], cc("rot"), raw[:, i % 2, :], start=True, stop=True))

                for i in range(4):
                    c = 1 + i // 2
                    if i % 2 == 0:
                        chunk_wait(l, c)
                    o = fill(l, f"raw{i}")
                    for j in range(2):
                        for k in range(KD):
                            m = pe.matmul(o[:, j * S:(j + 1) * S], W[c % 2][:, k, (2 * (i % 2) + j) * P:(2 * (i % 2) + j + 1) * P],
                                          xT[:, k, :], start=k == 0, stop=k == KD - 1)
                    filled(l, f"raw{i}", m)
                    if i:
                        rotate(i - 1)
                chunk_wait(l, 3)
                for t in range(NT):
                    o = fill(l, f"v{t}")
                    for k in range(KD):
                        m = pe.matmul(o[:, :], xT[:, k, t * P:(t + 1) * P], W[1][:, k, :],
                                      start=k == 0, stop=k == KD - 1)
                    filled(l, f"v{t}", m)
                    if t == 0:
                        rotate(3)
                chunk_wait(l, 4)
                o = fill(l, "u")
                for t in range(NT):
                    for k in range(KD):
                        m = pe.matmul(o[:, t * 256:(t + 1) * 256], xT[:, k, t * P:(t + 1) * P], W[0][:, k, 0:256],
                                      start=k == 0, stop=k == KD - 1)
                filled(l, "u", m)
                chunk_wait(l, 5)
                o = fill(l, "qm")
                for j in range(2):
                    for k in range(KD):
                        m = pe.matmul(o[:, j * S:(j + 1) * S], W[1][:, k, j * P:(j + 1) * P], xT[:, k, :],
                                      start=k == 0, stop=k == KD - 1)
                filled(l, "qm", m)
                pe.wait_ge(*read_at(l, "u"))
                pe.wait_ge(pool_in, 16 * l + 16)
                pe.wait_ge(small_in, 80 * l + 80)
                o = fill(l, "pooled")
                for g in range(4):
                    h0 = 64 * (g % 2)
                    for t in range(NT):
                        m = pe.matmul(o[h0:h0 + 64, (g // 2) * S:(g // 2 + 1) * S], uu[:, t, 64 * g:64 * g + 64],
                                      pool_sb[:, t, g, :], start=t == 0, stop=t == NT - 1)
                filled(l, "pooled", m)
                pe.wait_ge(*read_at(l, "pooled"))
                o = fill(l, "pmix")
                stand_alone(pe)
                for g in range(4):
                    h0 = 64 * (g % 2)
                    m = pe.matmul(o[h0:h0 + 64, (g // 2) * S:(g // 2 + 1) * S], wp[h0:h0 + 64, g // 2, :],
                                  pooledT[h0:h0 + 64, g // 2, :], start=True, stop=True)
                filled(l, "pmix", m)
                pe.wait_ge(qk_sb, 4 * l + 4)
                for name in ("qm", "v0", "v1", "kmT", "vm"):
                    pe.wait_ge(*read_at(l, name))

                def scores(u):
                    h0, c = 64 * (u % 2), u // 2
                    o = fill(l, f"s{u}")
                    if u < DSA_HEADS:
                        q, k = qkT[h0:h0 + 64, c, :], qkT[h0:h0 + 64, 4 + c, :]
                        pe.matmul(o[:, 0:P], q[:, 0:P], k[:, 0:P], start=True, stop=True)
                        m = pe.matmul(o[:, P:3 * P], q[:, P:S], k, start=True, stop=True)
                    else:
                        c -= 4
                        for t in range(NT):
                            m = pe.matmul(o[:, t * S:(t + 1) * S], qmT[h0:h0 + 64, c, t * P:(t + 1) * P],
                                          kmT[h0:h0 + 64, c, :], start=True, stop=True)
                    filled(l, f"s{u}", m)

                def turn_probs(u):
                    o = fill(l, f"pT{u}")
                    pe.wait_ge(p_rd, UNITS * l + u + 1)
                    src = (0, 1, 2) if u < DSA_HEADS else (0, 2, 1, 3)
                    for j, s_ in enumerate(src):
                        m = pe.transpose(o[:, j * P:(j + 1) * P], prob[:, u % 2, s_ * P:(s_ + 1) * P], ident)
                    filled(l, f"pT{u}", m)

                def outputs(u):
                    h0 = 64 * (u % 2)
                    o = bank[BANK_OF[f"o{u // 2}"]]
                    if u % 2 == 0:
                        fill(l, f"o{u // 2}")
                    pe.wait_ge(*read_at(l, f"pT{u}"))
                    pt = pT[:, u % 2, :]
                    if u < DSA_HEADS:
                        pe.matmul(o[h0:h0 + 64, 0:S], vv[:, 0, 64 * u:64 * u + 64], pt[:, 0:S], start=True, stop=False)
                        m = pe.matmul(o[h0:h0 + 64, P:S], vv[:, 1, 64 * u:64 * u + 64], pt[:, S:S + P], start=False, stop=True)
                    else:
                        h = u - DSA_HEADS
                        for t in range(2):
                            m = pe.matmul(o[h0:h0 + 64, 0:S], vm[:, t, 64 * h:64 * h + 64], pt[:, t * S:(t + 1) * S],
                                          start=t == 0, stop=t == 1)
                    if u % 2:
                        filled(l, f"o{u // 2}", m)
                scores(0)
                for u in range(UNITS + 1):
                    if u + 1 < UNITS:
                        scores(u + 1)
                    if u < UNITS:
                        turn_probs(u)
                    if u:
                        outputs(u - 1)
                for name in ["pmix"] + [f"o{c}" for c in range(UNITS // 2)]:
                    pe.wait_ge(*read_at(l, name))
                for half in range(2):
                    chunk_wait(l, 6 + half)
                    for t in range(NT):
                        name = f"wo{2 * half + t}"
                        o = fill(l, name)
                        for k in range(KD):
                            m = pe.matmul(o[:, :], mixT[:, k, t * P:(t + 1) * P], W[half][:, k, :],
                                          start=k == 0, stop=k == KD - 1)
                        filled(l, name, m)
                pe.wait_ge(x_ready, 2 * l + 2)
                transposes(l, "xTb", xs)
                for g in range(4):
                    pe.wait_ge(*read_at(l, f"xTb{g}"))
                o = fill(l, "logit")
                for t in range(NT):
                    for k in range(KD):
                        m = pe.matmul(o[:, t * E:(t + 1) * E], xT[:, k, t * P:(t + 1) * P], wr[:, k, :],
                                      start=k == 0, stop=k == KD - 1)
                filled(l, "logit", m)
                chunk_wait(l, 8)
                for t in range(NT):
                    o = fill(l, f"sh{t}")
                    for k in range(KD):
                        m = pe.matmul(o[:, :], xT[:, k, t * P:(t + 1) * P], W[0][:, k, :],
                                      start=k == 0, stop=k == KD - 1)
                    filled(l, f"sh{t}", m)
                o = fill(l, "cum")
                pe.wait_ge(chosen_rd, l + 1)
                ch = [chosenb[:, t * E:(t + 1) * E] for t in range(NT)]
                pe.matmul(o[:, 0:E], beforeb[:], ch[0], start=True, stop=True)
                pe.matmul(o[:, E:2 * E], onesb[:], ch[0], start=True, stop=False)
                pe.matmul(o[:, E:2 * E], beforeb[:], ch[1], start=False, stop=True)
                pe.matmul(o[:, 2 * E:3 * E], onesb[:], ch[0], start=True, stop=False)
                filled(l, "cum", pe.matmul(o[:, 2 * E:3 * E], onesb[:], ch[1], start=False, stop=True))
                o = fill(l, "shT")
                for t in range(NT):
                    pe.wait_ge(*read_at(l, f"sh{t}"))
                for t in range(NT):
                    for kc in range(KF):
                        m = pe.transpose(o[:, (2 * t + kc) * P:(2 * t + kc + 1) * P], hh[:, t, kc::KF], ident)
                filled(l, "shT", m)
                pe.wait_ge(*read_at(l, "shT"))
                chunk_wait(l, 9)
                wd = stage[:, 1, 0:KF * D].rearrange("p (k n) -> p k n", k=KF)
                for t in range(NT):
                    for half in range(2):
                        o = fill(l, f"acc{2 * t + half}")
                        for kc in range(KF):
                            m = pe.matmul(o[:, :], hT[:, (2 * t + kc) * P:(2 * t + kc + 1) * P],
                                          wd[:, kc, half * 512:(half + 1) * 512],
                                          start=kc == 0, stop=kc == KF - 1, skip_group_check=True)
                        filled(l, f"acc{2 * t + half}", m)
                pe.wait_ge(split_rd, 2 * l + 2)
                pe.wait_ge(route_rd, l + 1)
                passes(pe, l, run, skipped)

        @block.scalar
        def _(act):
            act.wait_ge(setup_done, 1)
            def copy(out_, in_, **kw):
                return act.activation(out_, in_, ACT.Copy, **kw)

            def take(l, name):
                act.wait_ge(*full_at(l, name))
                return bank[BANK_OF[name]]

            def evac(l, name, dst):
                copy(dst, take(l, name)[:, :]).then_inc(read[BANK_OF[name]], 1)

            def run(ps, base, round_):
                def g_half(n, half):
                    act.wait_ge(ps.g_full, 2 * n + half + 1)
                    copy(xg[:, 4 * half:4 * half + 4, :].rearrange("p k c -> p (k c)"), G[:, :]).then_inc(ps.g_sb, 1)
                g_half(base, 0)
                g_half(base, 1)

                def body(n, q, b, first, last):
                    act.wait_ge(ps.h_full, n + 1)
                    act.activation(sg[:, 0, :], H[:, 0:F], ACT.Silu).then_inc(ps.silu_rd, 1)
                    if not last:
                        g_half(n + 1, 0)
                        g_half(n + 1, 1)
                    act.wait_ge(ps.selT_sb, n + 1)
                    for half in range(2):
                        act.wait_ge(ps.y_full, 2 * n + half + 1)
                        copy(ysp[:, 0, half * 512:(half + 1) * 512], Y[half][:, :], scale=wslot[:, b:b + 1])\
                            .then_inc(ps.hi_rd, 1)
                    for half in range(2):
                        act.wait_ge(ps.res_rd, 2 * n + half + 1)
                        copy(ysp[:, 1, half * 512:(half + 1) * 512], yres[:, half * 512:(half + 1) * 512])\
                            .then_inc(ps.mid_rd, 1)
                pairs_of_pass(act, base, body)

            def skipped(n):
                for s_, k in ((more.g_sb, 2), (more.silu_rd, 1), (more.hi_rd, 2), (more.mid_rd, 2)):
                    act.sem_inc(s_, n * k)

            with act.Fori(0, DEPTH) as l:
                for g in (0, 2):
                    evac(l, f"xTa{g}", xT[:, 2 * g:2 * g + 2, :].rearrange("p k s -> p (k s)"))
                for g in (0, 2):
                    evac(l, f"memT{g}", memT[:, 2 * g:2 * g + 2, :].rearrange("p k s -> p (k s)"))
                evac(l, "kmT", kmT.rearrange("p k s -> p (k s)"))
                for i in range(4):
                    if i >= 2:
                        act.wait_ge(qk_sb, 4 * l + i - 1)
                    evac(l, f"raw{i}", raw[:, i % 2, :])
                evac(l, "v0", vv[:, 0, :])
                evac(l, "v1", vv[:, 1, :])
                evac(l, "u", uu.rearrange("p t n -> p (t n)"))
                evac(l, "qm", qmT.rearrange("p k s -> p (k s)"))

                def exps(u):
                    act.wait_ge(negm_rd, UNITS * l + u + 1)
                    if u < DSA_HEADS:
                        for t, a, z in ((0, 0, P), (1, P, 3 * P)):
                            m = act.activation(prob[:, u % 2, a:z], prob[:, u % 2, a:z], ACT.Exp,
                                               bias=negm[u % 2][:, t:t + 1], scale=SCALE)
                        m.then_inc(exp_rd, 1)
                    else:
                        if u >= 2:
                            act.wait_ge(*full_at(l, f"pT{u - 2}"))
                        s_ = take(l, f"s{u}")
                        for t in range(NT):
                            m = act.activation(prob[:, u % 2, t * S:(t + 1) * S], s_[:, t * S:(t + 1) * S], ACT.Exp,
                                               bias=negm[u % 2][:, t:t + 1], scale=SCALE,
                                               accum_out=den[u % 2][:, t:t + 1])
                        m.then_inc(read[BANK_OF[f"s{u}"]], 1)

                def turned(u):
                    w = 3 * P if u < DSA_HEADS else 4 * P
                    if u >= 2:
                        act.wait_ge(*full_at(l, f"o{(u - 2) // 2}"))
                    s_ = take(l, f"pT{u}")
                    copy(pT[:, u % 2, 0:w], s_[:, 0:w]).then_inc(read[BANK_OF[f"pT{u}"]], 1)
                for u in range(UNITS):
                    exps(u)
                    if u:
                        turned(u - 1)
                turned(UNITS - 1)

                def sqrt(i):
                    act.wait_ge(var_rd, 2 * l + i + 1)
                    act.activation(std, mv[:, :, 1], ACT.Sqrt, bias=epst[:, 0:1]).then_inc(std_rd, 1)
                sqrt(0)
                for g in (0, 2):
                    evac(l, f"xTb{g}", xT[:, 2 * g:2 * g + 2, :].rearrange("p k s -> p (k s)"))
                act.activation(sig, take(l, "logit")[:, 0:NT * E], ACT.Exp, scale=-1.0)\
                    .then_inc(read[BANK_OF["logit"]], 1)
                for t in range(NT):
                    copy(xsp[:, t, 0, :], xs[:, t, :]).then_inc(split_hi, 1)
                for t in range(NT):
                    act.wait_ge(*full_at(l, f"sh{t}"))
                    act.activation(sg[:, t, :], bank[BANK_OF[f"sh{t}"]][:, 0:F], ACT.Silu).then_inc(ssilu, 1)
                for t in range(NT):
                    act.wait_ge(split_rs, 2 * l + t + 1)
                    copy(xsp[:, t, 1, :], xres[:, t, :]).then_inc(split_hi, 1)
                passes(act, l, run, skipped)
                sqrt(1)

        @block.vector
        def _(dve):
            dve.memset(onesb[:], 1.0)
            dve.memset(epst[:], EPS)
            dve.memset(small[:], 0.0)
            dve.wait_ge(const_in, 16)
            dve.tensor_copy(identb[:], ident)
            dve.tensor_copy(beforeb[:], cc("before")).then_inc(setup_done, 1)
            for s_ in [*read, x_ready]:
                dve.sem_inc(s_, 1)
            dve.wait_ge(x_in, 16)
            links = [0]
            layer = [None]

            def link(ins):
                links[0] += 1
                ins.then_inc(dve_link, 1)
                dve.wait_ge(dve_link, layer[0] * DVE_LINKS + links[0])

            def take(l, name):
                dve.wait_ge(*full_at(l, name))
                return bank[BANK_OF[name]]

            def evac(l, name, dst):
                dve.tensor_copy(dst, take(l, name)[:, :]).then_inc(read[BANK_OF[name]], 1)

            def layer_norm(l, i, halves):
                for t in range(NT):
                    for h in range(2):
                        name = halves(t, h)
                        v = xs[:, t, h * 512:(h + 1) * 512]
                        m = dve.scalar_tensor_tensor(v, v, ALPHA, take(l, name)[:, :], ALU.mult, ALU.add)
                        m.then_inc(read[BANK_OF[name]], 1)
                        dve.wait_ge(*read_at(l, name))
                        m = dve.bn_stats(stats[:, t, h, :], v)
                link(m)
                stand_alone(dve)
                for t in range(NT):
                    m = dve.bn_aggr(mv[:, t, :], stats[:, t, :, :])
                m.then_inc(var_rd, 1)
                dve.wait_ge(std_rd, 2 * l + i + 1)
                link(dve.reciprocal(rstd, std))
                dve.wait_ge(ln_in, 64 * l + 32 * i + 32)
                for t in range(NT):
                    m = dve.tensor_scalar(xs[:, t, :], xs[:, t, :], mv[:, t, 0:1], rstd[:, t:t + 1], ALU.subtract, ALU.mult)
                link(m)
                for t in range(NT):
                    m = dve.tensor_tensor(xs[:, t, :], xs[:, t, :], lng, ALU.mult)
                link(m)
                for t in range(NT):
                    m = dve.tensor_tensor(xs[:, t, :], xs[:, t, :], lnb, ALU.add)
                m.then_inc(x_ready, 1)

            def run(ps, base, round_):
                if round_ is not None:
                    dve.tensor_scalar(pos, pos, -float(SLOTS), None, ALU.add).then_inc(pos_rd, 1)
                    dve.wait_ge(pos_rd, round_ + 1)
                slots = cc("slot").unsqueeze(1).to_broadcast([P, 2, SLOTS])
                posv = pos.rearrange("p (t r e) -> p t r e", t=NT, e=2)

                def build_sel(n, q, wait):
                    if wait:
                        dve.wait_ge(ps.selT_ps, n)
                    for t in range(NT):
                        m = dve.tensor_tensor(sel[:, t, :].rearrange("p (e c) -> p e c", e=2), slots,
                                              posv[:, t, q, :].unsqueeze(2).to_broadcast([P, 2, SLOTS]), ALU.is_equal)
                    m.then_inc(ps.sel_rd, 1)

                def take_selT(n, b):
                    dve.wait_ge(ps.selT_ps, n + 1)
                    dve.tensor_copy(selT[:, b, :], G[:].bitcast(BF16)[:, 0:S])
                    for e in range(2):
                        m = dve.tensor_reduce(wslot[64 * e:64 * e + 64, b:b + 1], G[64 * e:64 * e + 64, 256 + 3 * e:259 + 3 * e],
                                              AX.X, ALU.add)
                    m.then_inc(ps.selT_sb, 1)
                build_sel(base, 0, False)
                take_selT(base, 0)

                def body(n, q, b, first, last):
                    if not last:
                        build_sel(n + 1, q + 1, True)
                    dve.wait_ge(ps.silu_rd, n + 1)
                    dve.tensor_tensor(hh[:, 0, :], sg[:, 0, :], H[:, F:2 * F], ALU.mult).then_inc(ps.h_rd, 1)
                    dve.wait_ge(ps.hT_ps, n + 1)
                    dve.tensor_copy(hT[:, 0:F], H[:, 0:F]).then_inc(ps.hT_sb, 1)
                    dve.wait_ge(ps.selT_sb, n + 1)
                    if not first:
                        dve.wait_ge(ps.lo_rd, 2 * n)
                    for half in range(2):
                        dve.wait_ge(ps.hi_rd, 2 * n + half + 1)
                        dve.scalar_tensor_tensor(yres[:, half * 512:(half + 1) * 512], Y[half][:, :], wslot[:, b:b + 1],
                                                 ysp[:, 0, half * 512:(half + 1) * 512], ALU.mult, ALU.subtract)\
                            .then_inc(ps.res_rd, 1)
                    if not last:
                        take_selT(n + 1, 1 - b)
                    for half in range(2):
                        dve.wait_ge(ps.mid_rd, 2 * n + half + 1)
                        dve.tensor_tensor(ysp[:, 2, half * 512:(half + 1) * 512], yres[:, half * 512:(half + 1) * 512],
                                          ysp[:, 1, half * 512:(half + 1) * 512], ALU.subtract).then_inc(ps.lo_rd, 1)
                pairs_of_pass(dve, base, body)
                dve.wait_ge(ps.comb, base + PAIRS)

            def skipped(n):
                for s_, k in ((more.sel_rd, 1), (more.selT_sb, 1), (more.h_rd, 1), (more.hT_sb, 1),
                              (more.res_rd, 2), (more.lo_rd, 2)):
                    dve.sem_inc(s_, n * k)
                dve.sem_inc(pos_rd, n // PAIRS)

            with dve.Fori(0, DEPTH) as l:
                layer[0] = l
                links[0] = 0
                for g in (1, 3):
                    evac(l, f"xTa{g}", xT[:, 2 * g:2 * g + 2, :].rearrange("p k s -> p (k s)"))
                for g in (1, 3):
                    evac(l, f"memT{g}", memT[:, 2 * g:2 * g + 2, :].rearrange("p k s -> p (k s)"))
                evac(l, "vm", vm.rearrange("p k s -> p (k s)"))
                cos2 = cc("cos").unsqueeze(1).to_broadcast([P, 2, S])
                sin2 = cc("sin").unsqueeze(1).to_broadcast([P, 2, S])
                for i in range(4):
                    dve.wait_ge(*read_at(l, f"raw{i}"))
                    dst = qkT[:, 2 * i:2 * i + 2, :]
                    dve.tensor_tensor(dst, raw[:, i % 2, :].rearrange("p (c s) -> p c s", s=S), cos2, ALU.mult)
                    r_ = take(l, f"rot{i}")
                    if i:
                        dve.wait_ge(qk_sb, 4 * l + i)
                    m = dve.tensor_tensor(rt.rearrange("p (c s) -> p c s", s=S), r_[:, :].rearrange("p (c s) -> p c s", s=S),
                                          sin2, ALU.mult)
                    m.then_inc(read[BANK_OF[f"rot{i}"]], 1)
                    dve.wait_ge(*read_at(l, f"rot{i}"))
                    dve.tensor_tensor(dst, dst, rt.rearrange("p (c s) -> p c s", s=S), ALU.add).then_inc(qk_sb, 1)
                evac(l, "pooled", pooledT.rearrange("p k s -> p (k s)"))
                dve.wait_ge(small_in, 80 * l + 80)
                o = take(l, "pmix")
                for j in range(2):
                    m = dve.tensor_scalar(mixT[:, j, :], o[:, j * S:(j + 1) * S], psc[:, j:j + 1], None, ALU.mult)
                m.then_inc(read[BANK_OF["pmix"]], 1)

                def maxima(u):
                    i = u % 2
                    o = take(l, f"s{u}")
                    if u < DSA_HEADS:
                        if u >= 2:
                            dve.wait_ge(*full_at(l, f"pT{u - 2}"))
                        stand_alone(dve)
                        for t, a, z in ((0, 0, P), (1, P, 3 * P)):
                            m = dve.tensor_tensor_reduce(prob[:, i, a:z], o[:, a:z], cc("bias")[:, a:z], 1.0, -3e38,
                                                         ALU.add, ALU.max, mx[i][:, t:t + 1])
                        m.then_inc(read[BANK_OF[f"s{u}"]], 1)
                        dve.wait_ge(*read_at(l, f"s{u}"))
                    else:
                        link(dve.tensor_reduce(mx[i], o[:, :].rearrange("p (t s) -> p t s", t=NT), AX.X, ALU.max))
                    dve.tensor_scalar(negm[i], mx[i], -SCALE, None, ALU.mult).then_inc(negm_rd, 1)

                def normalise(u):
                    i = u % 2
                    if u < DSA_HEADS:
                        dve.wait_ge(exp_rd, DSA_HEADS * l + u + 1)
                    else:
                        dve.wait_ge(*read_at(l, f"s{u}"))
                    cuts = ((0, 0, P), (1, P, 3 * P)) if u < DSA_HEADS else ((0, 0, S), (1, S, 2 * S))
                    if u < DSA_HEADS:
                        for t, a, z in cuts:
                            m = dve.tensor_tensor_reduce(prob[:, i, a:z], prob[:, i, a:z], cc("mult")[:, a:z], 1.0, 0.0,
                                                         ALU.mult, ALU.add, den[i][:, t:t + 1])
                        link(m)
                    link(dve.reciprocal(rden[i], den[i]))
                    for t, a, z in cuts:
                        m = dve.tensor_scalar(prob[:, i, a:z], prob[:, i, a:z], rden[i][:, t:t + 1], None, ALU.mult)
                    m.then_inc(p_rd, 1)

                def heads_out(c):
                    name = f"o{c}"
                    m = dve.tensor_copy(mixT[:, 2 + c, :], take(l, name)[:, 0:S])
                    m.then_inc(read[BANK_OF[name]], 1)
                maxima(0)
                for u in range(UNITS):
                    if u + 1 < UNITS:
                        maxima(u + 1)
                    normalise(u)
                    if u >= 3 and u % 2:
                        heads_out((u - 3) // 2)
                heads_out(UNITS // 2 - 1)
                layer_norm(l, 0, lambda t, h: f"wo{2 * h + t}")

                for g in (1, 3):
                    evac(l, f"xTb{g}", xT[:, 2 * g:2 * g + 2, :].rearrange("p k s -> p (k s)"))
                dve.wait_ge(*read_at(l, "logit"))
                link(dve.tensor_scalar(sig, sig, 1.0, None, ALU.add))
                link(dve.reciprocal(sig, sig))
                link(dve.tensor_tensor(biased.rearrange("p (t e) -> p t e", t=NT), sig.rearrange("p (t e) -> p t e", t=NT),
                                       rb[:].unsqueeze(1).to_broadcast([P, NT, E]), ALU.add))
                stand_alone(dve)
                for j in range(NT * GROUPS):
                    m = dve.max(g8[:, 8 * j:8 * j + 8], biased[:, 8 * j:8 * j + 8])
                link(m)
                g8v = g8.rearrange("p (j k) -> p j k", k=8)
                link(dve.tensor_tensor(gs, g8v[:, :, 0], g8v[:, :, 1], ALU.add))
                for t in range(NT):
                    v = gs[:, t * GROUPS:(t + 1) * GROUPS]
                    other = v.unsqueeze(1).to_broadcast([P, GROUPS, GROUPS])
                    own = v.unsqueeze(2).to_broadcast([P, GROUPS, GROUPS])
                    c1 = cmp1.rearrange("p (i j) -> p i j", j=GROUPS)
                    c2 = cmp2.rearrange("p (i j) -> p i j", j=GROUPS)
                    dve.tensor_tensor(c1, other, own, ALU.is_gt)
                    link(dve.tensor_tensor(c2, other, own, ALU.is_equal))
                    link(dve.tensor_tensor(cmp2, cmp2, cc("tri"), ALU.mult))
                    link(dve.tensor_tensor(cmp1, cmp1, cmp2, ALU.add))
                    link(dve.tensor_reduce(rank[:, t * GROUPS:(t + 1) * GROUPS], c1, AX.X, ALU.add))
                link(dve.tensor_scalar(rank, rank, float(TOP_GROUPS), None, ALU.is_lt))
                link(dve.tensor_scalar(gneg, rank, BIG, -BIG, ALU.mult, ALU.add))
                b3 = biased.rearrange("p (j k) -> p j k", k=8)
                m3 = masked.rearrange("p (j k) -> p j k", k=8)
                link(dve.tensor_tensor(m3, b3, rank.unsqueeze(2).to_broadcast([P, NT * GROUPS, 8]), ALU.mult))
                link(dve.tensor_tensor(m3, m3, gneg.unsqueeze(2).to_broadcast([P, NT * GROUPS, 8]), ALU.add))
                stand_alone(dve)
                for t in range(NT):
                    m = dve.max(top[:, 8 * t:8 * t + 8], masked[:, t * E:(t + 1) * E])
                link(m)
                stand_alone(dve)
                for t in range(NT):
                    m = dve.match_replace(chosen[:, t * E:(t + 1) * E], top[:, 8 * t:8 * t + 8],
                                          masked[:, t * E:(t + 1) * E], GONE)
                link(m)
                link(dve.tensor_scalar(chosen, chosen, GONE / 2, None, ALU.is_lt))
                dve.tensor_copy(chosenb, chosen).then_inc(chosen_rd, 1)
                for t in range(NT):
                    m = dve.tensor_tensor_reduce(wts[:, t * E:(t + 1) * E], chosen[:, t * E:(t + 1) * E],
                                                 sig[:, t * E:(t + 1) * E], 1.0, 0.0, ALU.mult, ALU.add, wsum[:, t:t + 1])
                link(m)
                link(dve.reciprocal(wrec, wsum))
                for t in range(NT):
                    m = dve.tensor_scalar(wts[:, t * E:(t + 1) * E], wts[:, t * E:(t + 1) * E], wrec[:, t:t + 1],
                                          ROUTED_SCALE, ALU.mult, ALU.mult)
                link(m)
                wp_ = [w3[:, :, :, s_] for s_ in range(3)]
                wv = wts.rearrange("p (t e) -> p t e", t=NT)
                wrv = wres.rearrange("p (t e) -> p t e", t=NT)
                link(dve.tensor_copy(wp_[0], wv))
                link(dve.tensor_tensor(wrv, wv, wp_[0], ALU.subtract))
                link(dve.tensor_copy(wp_[1], wrv))
                dve.tensor_tensor(wp_[2], wrv, wp_[1], ALU.subtract)
                o = take(l, "cum")
                link(dve.scalar_tensor_tensor(pos, o[:, 0:NT * E], 1.0, chosen, ALU.add, ALU.mult))
                dve.tensor_scalar(pos, pos, -1.0, None, ALU.add)
                m = dve.tensor_reduce(cntf, o[:, NT * E:(NT + 1) * E], AX.X, ALU.max)
                m.then_inc(read[BANK_OF["cum"]], 1)
                dve.wait_ge(*read_at(l, "cum"))
                dve.tensor_copy(counts_i[:], cntf).then_inc(route_rd, 1)
                for t in range(NT):
                    dve.wait_ge(split_hi, 4 * l + t + 1)
                    dve.tensor_tensor(xres[:, t, :], xs[:, t, :], xsp[:, t, 0, :], ALU.subtract).then_inc(split_rs, 1)
                for t in range(NT):
                    dve.wait_ge(ssilu, 2 * l + t + 1)
                    name = f"sh{t}"
                    m = dve.tensor_tensor(hh[:, t, :], sg[:, t, :], take(l, name)[:, F:2 * F], ALU.mult)
                    m.then_inc(read[BANK_OF[name]], 1)
                evac(l, "shT", hT)
                for t in range(NT):
                    dve.wait_ge(split_hi, 4 * l + 2 + t + 1)
                    dve.tensor_tensor(xsp[:, t, 2, :], xres[:, t, :], xsp[:, t, 1, :], ALU.subtract).then_inc(split_rd, 1)
                dve.wait_ge(split_rd, 2 * l + 2)
                passes(dve, l, run, skipped)
                layer_norm(l, 1, lambda t, h: f"acc{2 * t + h}")
                assert links[0] == DVE_LINKS, links[0]


_INS = ["x", "mem", "w_in", "w_pool", "pool_scale", "w_mem_kv", "w_out", "ln1_g", "ln1_b", "w_router",
        "router_bias", "w_gate", "w_up", "w_down", "ws_gate", "ws_up", "ws_down", "ln2_g", "ln2_b"]


def kernel(**inputs):
    import concourse.bacc as bacc
    from concourse.bass_utils import run_bass_kernel_spmd

    nc = bacc.Bacc("TRN2", target_bir_lowering=False, num_devices=1)
    consts, pool_mat = constants()
    given = {n: np.ascontiguousarray(inputs[n]) for n in _INS}
    given["consts"], given["pool_mat"] = consts, pool_mat
    arrays, args = {}, []
    for name, a in given.items():
        arrays[f"in_{name}"] = a
        args.append(nc.dram_tensor(f"in_{name}", a.shape, mybir.dt.from_np(a.dtype), kind="ExternalInput").ap())
    args.append(nc.dram_tensor("out_x", (1, S, D), F32, kind="ExternalOutput").ap())
    build(nc, *args)
    r = run_bass_kernel_spmd(nc, [arrays], core_ids=[0])
    return r.results[0]["out_x"]
```

```python
from contextlib import ExitStack

import numpy as np
import concourse.bass as bass
from concourse import mybir

F32 = mybir.dt.float32
BF16 = mybir.dt.bfloat16
I32 = mybir.dt.int32
ALU = mybir.AluOpType
ACT = mybir.ActivationFunctionType
AX = mybir.AxisListType

P = 128
DEPTH, D, S = 2, 1024, 256
NT = S // P
KD = D // P
HD = 64
DSA_HEADS, MEM_HEADS = 8, 4
SCALE = HD ** -0.5
WINDOWS = (2, 4, 8, 16)
PATTERNS = ((128, 1), (512, 4), (2048, 16))
ROT = HD // 4
POOL_W = D // 4
E, TOPK, GROUPS, TOP_GROUPS = 64, 8, 8, 4
F = 256
KF = F // P
SLOTS = 64
PAIRS = E // 2
ROUNDS = S // SLOTS
ROUTED_SCALE = 2.5
ALPHA = float((2 * DEPTH) ** 0.25)
EPS = 1e-5
BIG = 1e30
GONE = -3e38

CONSTS = {}
_at = 0
for _n, _w in (("ident", P), ("rot", P), ("before", P), ("slot", SLOTS), ("tri", GROUPS * GROUPS),
               ("cos", S), ("sin", S), ("bias", 3 * P), ("mult", 3 * P)):
    CONSTS[_n] = (_at, _at + _w)
    _at += _w
NCONST = _at


def constants():
    c = np.zeros((P, NCONST), np.float32)

    def put(name, v):
        c[:, CONSTS[name][0]:CONSTS[name][1]] = v
    i, j = np.arange(P)[:, None], np.arange(P)[None]
    put("ident", i == j)
    put("before", i < j)
    put("slot", np.arange(SLOTS)[None])
    g = np.arange(GROUPS)
    put("tri", (g[None, :] < g[:, None]).reshape(1, -1))
    half = ROT // 2
    r = np.zeros((P, P))
    for h in range(0, P, HD):
        for d in range(half):
            r[h + d + half, h + d] = -1
            r[h + d, h + d + half] = 1
    put("rot", r)
    inv = np.float32(500000.0) ** (-np.arange(0, ROT, 2, dtype=np.float32) / np.float32(ROT))
    ang = np.arange(S, dtype=np.float32)[:, None] * inv[None]
    cos, sin = np.ones((P, S)), np.zeros((P, S))
    for h in range(0, P, HD):
        for d in range(ROT):
            cos[h + d] = np.cos(ang[:, d % half])
            sin[h + d] = np.sin(ang[:, d % half])
    put("cos", cos)
    put("sin", sin)
    qi, kj = np.arange(S)[:, None], np.arange(S)[None]
    m = np.zeros((S, S))
    for window, dil in PATTERNS:
        d = qi - kj
        m += (d >= 0) & (d % dil == 0) & (d // dil <= window // dil)
    m = np.concatenate([m[:P, :P], m[P:]], axis=1)
    put("mult", m)
    put("bias", np.where(m > 0, 0.0, -BIG))
    s = np.arange(S)
    pool = np.zeros((S, len(WINDOWS), S), np.float32)
    for n, w in enumerate(WINDOWS):
        inside = (qi <= s[None]) & (qi > s[None] - w)
        pool[:, n] = inside / np.minimum(s + 1, w)[None] - (qi == s[None])
    pool = pool.reshape(NT, P, -1).transpose(1, 0, 2).reshape(P, -1)
    return c, np.ascontiguousarray(pool.astype(np.float32))


UNITS = DSA_HEADS + MEM_HEADS
FILLS = ([(f"memT{g}", 4 + g) for g in range(4)] + [("kmT", 4), ("vm", 5)]
         + [(f"xTa{g}", g) for g in range(4)]
         + [(f"{a}{i}", (2 if a == "raw" else 6) + i % 2) for i in range(4) for a in ("raw", "rot")]
         + [("v0", 0), ("v1", 1)])
for _u in range(UNITS):
    FILLS += [(f"s{_u}", 4 + _u % 2)]
    FILLS += {0: [("u", 2)], 2: [("qm", 3)], 4: [("pooled", 2)], 5: [("pmix", 3)],
              6: [("wo0", 2)], 7: [("wo1", 3)]}.get(_u, [])
    FILLS += [(f"pT{_u}", 6 + _u % 2)]
    if _u % 2:
        FILLS += [(f"o{_u // 2}", (_u // 2) % 2)]
FILLS += [("wo2", 4), ("wo3", 5)]
FILLS += [(f"xTb{g}", (6, 7, 0, 1)[g]) for g in range(4)]
FILLS += [("logit", 2), ("sh0", 4), ("cum", 3), ("sh1", 5), ("shT", 6)]
FILLS += [(f"acc{i}", i) for i in range(4)]
PER_BANK = [sum(b == n for _, b in FILLS) for n in range(8)]
BANK_OF = dict(FILLS)
ORDER = {name: sum(b == bank for _, b in FILLS[:i]) for i, (name, bank) in enumerate(FILLS)}

CHUNKS = ["kv", "mem", "q", "k", "v", "uqm", "wo0", "wo1", "sgu", "sd"]
LAST_USE = ["vm", "memT3", "raw1", "raw3", "v1", "qm", "wo2", "wo3", "sh1", "acc3"]
NCH = len(CHUNKS)
DVE_LINKS = 59


def build(nc, x, mem, w_in, w_pool, pool_scale, w_mem_kv, w_out, ln1_g, ln1_b, w_router,
          router_bias, w_gate, w_up, w_down, ws_gate, ws_up, ws_down, ln2_g, ln2_b,
          consts, pool_mat, out):
    with ExitStack() as ctx:
        def sb(name, shape, dt=F32):
            return ctx.enter_context(nc.sbuf_tensor(name, shape, dt))

        def sem(name):
            return ctx.enter_context(nc.semaphore(name))

        bank = [ctx.enter_context(nc.psum_tensor(f"bank{i}", [P, 512], F32)) for i in range(8)]
        acc = bank[0:4]
        G, H, Y = bank[4], bank[5], bank[6:8]

        gu = sb("gu", [P, 2, 2, 2, KD, F])
        dn = sb("dn", [P, 2, 2, KF, D])
        stage = sb("stage", [P, 2, KD * 512])
        xs = sb("xs", [P, NT, D])
        xT = sb("xT", [P, KD, S])
        cst = sb("cst", [P, NCONST])
        r8 = sb("r8", [P, 2048])
        small = sb("small", [P, 64])
        identb = sb("identb", [P, P], BF16)
        beforeb = sb("beforeb", [P, P], BF16)
        onesb = sb("onesb", [P, P], BF16)
        wr = sb("wr", [P, KD, E])
        rb = sb("rb", [P, E])
        wp = sb("wp", [P, 2, HD])
        psc = sb("psc", [P, 2])
        epst = sb("epst", [P, 1])
        scratch = sb("scratch", [P, 10752])
        off = [0]

        def part(n, dt=F32):
            v = scratch[:, off[0]:off[0] + n]
            off[0] += n
            assert off[0] <= 10752, off[0]
            return v if dt == F32 else v.bitcast(dt)
        qkT = part(8 * S).rearrange("p (c s) -> p c s", s=S)
        vv = part(NT * 512).rearrange("p (t n) -> p t n", t=NT)
        qmT = part(2 * S).rearrange("p (c s) -> p c s", s=S)
        kmT = part(2 * S).rearrange("p (c s) -> p c s", s=S)
        vm = part(2 * S).rearrange("p (t n) -> p t n", t=2)
        mixT = part(KD * S).rearrange("p (c s) -> p c s", s=S)
        uu = part(NT * 256).rearrange("p (t n) -> p t n", t=NT)
        pooledT = part(2 * S).rearrange("p (c s) -> p c s", s=S)
        raw = part(2 * 512).rearrange("p (b n) -> p b n", b=2)
        rt = part(512)
        pT = part(2 * 512).rearrange("p (b n) -> p b n", b=2)
        memT = mixT
        off[0] = 0
        xsp = part(NT * 3 * D // 2, BF16).rearrange("p (t s d) -> p t s d", t=NT, s=3)
        xres = part(NT * D).rearrange("p (t d) -> p t d", t=NT)
        ysp = part(3 * D // 2, BF16).rearrange("p (s d) -> p s d", s=3)
        xg = part(KD * P).rearrange("p (k c) -> p k c", k=KD)
        hh = part(2 * F).rearrange("p (t n) -> p t n", t=NT)
        hT = part(2 * F)
        sg = part(2 * F).rearrange("p (t n) -> p t n", t=NT)
        sel = part(NT * P // 2, BF16).rearrange("p (t c) -> p t c", t=NT)
        selT = part(2 * S // 2, BF16).rearrange("p (b s) -> p b s", b=2)
        pos = part(NT * E)
        w3 = part(NT * E * 3 // 2, BF16).rearrange("p (t e s) -> p t e s", t=NT, s=3)
        off[0] = NT * 3 * D // 2 + NT * D
        sig = part(NT * E)
        biased = part(NT * E)
        masked = part(NT * E)
        chosen = part(NT * E)
        wts = part(NT * E)
        wres = part(NT * E)
        chosenb = part(NT * E // 2, BF16)
        g8 = part(NT * GROUPS * 8)
        gs = part(NT * GROUPS)
        cmp1 = part(GROUPS * GROUPS)
        cmp2 = part(GROUPS * GROUPS)
        rank = part(NT * GROUPS)
        gneg = part(NT * GROUPS)
        top = part(NT * 8)
        assert off[0] <= NT * 3 * D // 2 + NT * D + 3 * D // 2
        counts_i = sb("counts_i", [P, 1], I32)
        yres = xres[:, 0, :]

        def cc(name):
            return cst[:, CONSTS[name][0]:CONSTS[name][1]]
        ident = cc("ident")
        mem_sb = stage[:, 1, 0:2 * D].rearrange("p (t d) -> p t d", t=2)
        pool_sb = r8[:].rearrange("p (t g s) -> p t g s", t=NT, g=len(WINDOWS))
        prob = raw
        lng, lnb = r8[:, 0:D], r8[:, D:2 * D]

        mx = [small[:, 0:2], small[:, 2:4]]
        negm = [small[:, 4:6], small[:, 6:8]]
        den = [small[:, 8:10], small[:, 10:12]]
        rden = [small[:, 12:14], small[:, 14:16]]
        mv = small[:, 16:20].rearrange("p (t n) -> p t n", t=NT)
        std = small[:, 20:22]
        rstd = small[:, 22:24]
        stats = small[:, 24:48].rearrange("p (t h n) -> p t h n", t=NT, h=2)
        wsum = small[:, 48:50]
        wrec = small[:, 50:52]
        wslot = small[:, 52:54]
        cntf = small[:, 54:55]

        full = [sem(f"bank{i}_full") for i in range(8)]
        read = [sem(f"bank{i}_read") for i in range(8)]
        const_in = sem("const_in")
        carried = sem("carried")
        x_in = sem("x_in")
        setup_done = sem("setup_done")
        small_in = sem("small_in")
        pool_in = sem("pool_in")
        ln_in = sem("ln_in")
        chunk_in = [sem(f"chunk_in{i}") for i in range(2)]
        x_ready = sem("x_ready")
        qk_sb = sem("qk_sb")
        negm_rd = sem("negm_rd")
        exp_rd = sem("exp_rd")
        p_rd = sem("p_rd")
        var_rd = sem("var_rd")
        std_rd = sem("std_rd")
        chosen_rd = sem("chosen_rd")
        route_rd = sem("route_rd")
        split_hi = sem("split_hi")
        split_rs = sem("split_rs")
        split_rd = sem("split_rd")
        ssilu = sem("ssilu")
        pos_rd = sem("pos_rd")
        dve_link = sem("dve_link")
        out_done = sem("out_done")

        class Pass:

            def __init__(self, tag, per_layer):
                self.per_layer = per_layer
                self.sel_rd = sem(f"{tag}_sel_rd")
                self.g_full = sem(f"{tag}_g_full")
                self.g_sb = sem(f"{tag}_g_sb")
                self.selT_ps = sem(f"{tag}_selT_ps")
                self.selT_sb = sem(f"{tag}_selT_sb")
                self.h_full = sem(f"{tag}_h_full")
                self.silu_rd = sem(f"{tag}_silu_rd")
                self.h_rd = sem(f"{tag}_h_rd")
                self.hT_ps = sem(f"{tag}_hT_ps")
                self.hT_sb = sem(f"{tag}_hT_sb")
                self.y_full = sem(f"{tag}_y_full")
                self.hi_rd = sem(f"{tag}_hi_rd")
                self.res_rd = sem(f"{tag}_res_rd")
                self.mid_rd = sem(f"{tag}_mid_rd")
                self.lo_rd = sem(f"{tag}_lo_rd")
                self.comb = sem(f"{tag}_comb")
        main = Pass("main", PAIRS)
        more = Pass("more", PAIRS * (ROUNDS - 1))
        gu_in = [sem(f"gu_in{b}") for b in range(2)]
        dn_in = [sem(f"dn_in{b}") for b in range(2)]
        mgu_in = [sem(f"mgu_in{b}") for b in range(2)]
        mdn_in = [sem(f"mdn_in{b}") for b in range(2)]
        main.w_in = (gu_in, dn_in)
        more.w_in = (mgu_in, mdn_in)

        block = ctx.enter_context(nc.Block())

        def stand_alone(eng):
            eng.sem_inc(carried, 1)

        def x_at(l, i, t):
            return x_ready, 4 * l + 2 * i + t + 2

        def x_before(l):
            return x_ready, 4 * l + 1

        def full_at(l, name):
            b = BANK_OF[name]
            return full[b], l * PER_BANK[b] + ORDER[name] + 1

        def read_at(l, name):
            b = BANK_OF[name]
            return read[b], l * PER_BANK[b] + ORDER[name] + 2

        def free_at(l, name):
            b = BANK_OF[name]
            return read[b], l * PER_BANK[b] + ORDER[name] + 1

        def pairs_of_pass(eng, base, body):
            for b in range(2):
                body(base + b, b, b, b == 0, False)
            with eng.Fori(1, PAIRS // 2 - 1) as i:
                for b in range(2):
                    body(base + 2 * i + b, 2 * i + b, b, False, False)
            for b in range(2):
                q = PAIRS - 2 + b
                body(base + q, q, b, False, b == 1)

        def passes(eng, l, run, skipped):
            run(main, l * PAIRS, None)
            eng.wait_ge(route_rd, l + 1)
            stand_alone(eng)
            cnt = eng.value_load(counts_i[0:1, 0:1], min_val=0, max_val=S)
            with eng.If(cnt > SLOTS):
                eng.wait_ge(main.comb, l * PAIRS + PAIRS)
                stand_alone(eng)
                with eng.Fori(0, ROUNDS - 1) as r:
                    run(more, l * more.per_layer + r * PAIRS, l * (ROUNDS - 1) + r)
                eng.nop()
            with eng.Else():
                skipped(more.per_layer)
                eng.nop()

        @block.sync
        def _(sp):
            sp.dma_start(xs[:], x[0].rearrange("(t p) d -> p t d", p=P)).then_inc(x_in, 16)
            sp.dma_start(cst[:], consts).then_inc(const_in, 16)
            kvv = w_mem_kv.rearrange("l (p k) n -> l p k n", k=KD)
            win = w_in.rearrange("l (p k) n -> l p k n", k=KD)
            wov = w_out.rearrange("l (k p) n -> l p k n", p=P)
            sgv = ws_gate.rearrange("l (p k) n -> l p k n", k=KD)
            suv = ws_up.rearrange("l (p k) n -> l p k n", k=KD)
            sdv = ws_down.rearrange("l (p k) n -> l p k n", k=KF)
            gv = w_gate.rearrange("l (r e) (p k) n -> (l r) p e (k n)", e=2, k=KD)
            uv = w_up.rearrange("l (r e) (p k) n -> (l r) p e (k n)", e=2, k=KD)
            dv = w_down.rearrange("l (r e) (p k) n -> (l r) p e (k n)", e=2, k=KF)

            def chunk(l, c):
                half = c % 2
                if c >= 2:
                    sp.wait_ge(*full_at(l, LAST_USE[c - 2]))
                dst = stage[:, half, :].rearrange("p (k n) -> p k n", k=KD)
                name = CHUNKS[c]
                stand_alone(sp)
                s_in = chunk_in[half]
                if name == "sgu":
                    sp.dma_start(dst[:, :, 0:256], sgv[l]).then_inc(s_in, 16)
                    sp.dma_start(dst[:, :, 256:512], suv[l]).then_inc(s_in, 16)
                elif name == "mem":
                    for t in range(2):
                        sp.dma_start(mem_sb[:, t, :], mem[0, t * P:(t + 1) * P, :]).then_inc(s_in, 16)
                elif name == "uqm":
                    for j, at in ((0, 0), (1, POOL_W + 3 * 512)):
                        sp.dma_start(dst[:, :, j * 256:(j + 1) * 256], win[l][:, :, at:at + 256]).then_inc(s_in, 16)
                else:
                    if name == "kv":
                        src = kvv[l]
                    elif name in ("q", "k", "v"):
                        at = POOL_W + 512 * "qkv".index(name)
                        src = win[l][:, :, at:at + 512]
                    elif name in ("wo0", "wo1"):
                        at = 512 * int(name[2])
                        src = wov[l][:, :, at:at + 512]
                    else:
                        src, dst = sdv[l], stage[:, half, 0:KF * D].rearrange("p (k n) -> p k n", k=KF)
                    cut = src.shape[1] // 2
                    sp.dma_start(dst[:, 0:cut], src[:, 0:cut]).then_inc(s_in, 16)
                    sp.dma_start(dst[:, cut:], src[:, cut:]).then_inc(s_in, 16)

            def pair(ps, l, n, q, b, first, at_start):
                if not at_start:
                    sp.wait_ge(ps.h_full, n - 1)
                r = l * PAIRS + q
                gu_s, dn_s = ps.w_in
                sp.dma_start(gu[:, b, :, 0, :, :].rearrange("p e k n -> p e (k n)"), gv[r]).then_inc(gu_s[b], 16)
                sp.dma_start(gu[:, b, :, 1, :, :].rearrange("p e k n -> p e (k n)"), uv[r]).then_inc(gu_s[b], 16)
                if not at_start:
                    sp.wait_ge(ps.y_full, 2 * n - 2)
                sp.dma_start(dn[:, b].rearrange("p e k n -> p e (k n)"), dv[r]).then_inc(dn_s[b], 16)

            with sp.Fori(0, DEPTH) as l:
                chunk(l, 0)
                chunk(l, 1)
                sp.wait_ge(*x_before(l))
                sp.dma_start(wr[:], w_router.rearrange("l (p k) e -> l p k e", k=KD)[l]).then_inc(small_in, 16)
                sp.dma_start(rb[:], router_bias.rearrange("l (o e) -> l o e", o=1)[l].to_broadcast([P, E])).then_inc(small_in, 16)
                for g2 in range(2):
                    sp.dma_start(wp[64 * g2:64 * g2 + 64], w_pool.rearrange("l (j h) c d -> l h c j d", h=2)[l, g2]).then_inc(small_in, 16)
                sp.dma_start(psc[:], pool_scale.rearrange("l (j p) -> l p j", p=P)[l], allow_slow_non_contiguous=True).then_inc(small_in, 16)
                sp.dma_start(r8[:], pool_mat).then_inc(pool_in, 16)
                for c in range(2, 6):
                    chunk(l, c)
                pair(main, l, None, 0, 0, True, True)
                chunk(l, 6)
                chunk(l, 7)
                pair(main, l, None, 1, 1, True, True)
                sp.wait_ge(*full_at(l, "pooled"))
                sp.dma_start(lng, ln1_g.rearrange("l (o d) -> l o d", o=1)[l].to_broadcast([P, D])).then_inc(ln_in, 16)
                sp.dma_start(lnb, ln1_b.rearrange("l (o d) -> l o d", o=1)[l].to_broadcast([P, D])).then_inc(ln_in, 16)
                chunk(l, 8)
                chunk(l, 9)
                sp.wait_ge(*x_at(l, 0, NT - 1))
                sp.dma_start(lng, ln2_g.rearrange("l (o d) -> l o d", o=1)[l].to_broadcast([P, D])).then_inc(ln_in, 16)
                sp.dma_start(lnb, ln2_b.rearrange("l (o d) -> l o d", o=1)[l].to_broadcast([P, D])).then_inc(ln_in, 16)

                def run(ps, base, round_):
                    if round_ is not None:
                        for b in range(2):
                            pair(ps, l, None, b, b, True, True)
                    with sp.Fori(1, PAIRS // 2) as i:
                        for b in range(2):
                            pair(ps, l, base + 2 * i + b, 2 * i + b, b, False, False)
                    if round_ is not None:
                        sp.wait_ge(ps.comb, base + PAIRS)
                        stand_alone(sp)

                def skipped(n):
                    for s_, k in ((mgu_in, 16), (mdn_in, 8)):
                        for b in range(2):
                            sp.sem_inc(s_[b], n * k)
                passes(sp, l, run, skipped)
            sp.wait_ge(*x_before(DEPTH))
            sp.dma_start(out[0].rearrange("(t p) d -> p t d", p=P), xs[:]).then_inc(out_done, 16)
            sp.wait_ge(out_done, 16)

        @block.tensor
        def _(pe):
            pe.wait_ge(const_in, 16)
            pe.wait_ge(x_in, 16)
            pe.wait_ge(setup_done, 1)
            layer = [None]

            def fill(l, name):
                pe.wait_ge(*free_at(l, name))
                return bank[BANK_OF[name]]

            def filled(l, name, ins):
                ins.then_inc(full[BANK_OF[name]], 1)

            def chunk_wait(l, c):
                pe.wait_ge(chunk_in[c % 2], l * (32 * NCH // 2) + 32 * (c // 2 + 1))

            def transposes(l, tag, src, tile_ready):
                for t in range(NT):
                    for w in tile_ready(t):
                        pe.wait_ge(*w)
                    for g in range(4):
                        o = fill(l, f"{tag}{g}") if t == 0 else bank[BANK_OF[f"{tag}{g}"]]
                        for kk in range(2):
                            m = pe.transpose(o[:, kk * S + t * P:kk * S + t * P + P], src[:, t, 2 * g + kk::KD], ident)
                        if t == NT - 1:
                            filled(l, f"{tag}{g}", m)

            def gather(ps, n, half, g_free):
                for w in g_free:
                    pe.wait_ge(*w)
                for kk in range(4):
                    k = 4 * half + kk
                    for j in range(3 * NT):
                        t, s = j // 3, j % 3
                        m = pe.matmul(G[:, kk * P:(kk + 1) * P], xsp[:, t, s, k::KD], sel[:, t, :],
                                      start=j == 0, stop=j == 3 * NT - 1)
                m.then_inc(ps.g_full, 1)

            def turn_sel(ps, n, q):
                pe.wait_ge(ps.g_sb, 2 * n + 2)
                gb = G[:].bitcast(BF16)
                for t in range(NT):
                    pe.transpose(gb[:, t * P:(t + 1) * P], sel[:, t, :], identb[:])
                for t in range(NT):
                    wq = w3[:, t].rearrange("p (r e) s -> p r (e s)", e=2)
                    m = pe.matmul(G[:, 256:262], sel[:, t, :], wq[:, q, :],
                                  start=t == 0, stop=t == NT - 1)
                m.then_inc(ps.selT_ps, 1)

            def combine(ps, n, b):
                pe.wait_ge(ps.lo_rd, 2 * n + 2)
                for t in range(NT):
                    for half in range(2):
                        for s in range(3):
                            m = pe.matmul(acc[2 * t + half][:, :], selT[:, b, t * P:(t + 1) * P],
                                          ysp[:, s, half * 512:(half + 1) * 512],
                                          start=False, stop=False, skip_group_check=True)
                m.then_inc(ps.comb, 1)

            def shared_turn(l):
                o = fill(l, "shT")
                for t in range(NT):
                    pe.wait_ge(*read_at(l, f"sh{t}"))
                    for kc in range(KF):
                        m = pe.transpose(o[:, (2 * t + kc) * P:(2 * t + kc + 1) * P], hh[:, t, kc::KF], ident)
                filled(l, "shT", m)

            def shared_down(l):
                pe.wait_ge(*read_at(l, "shT"))
                chunk_wait(l, 9)
                wd = stage[:, 1, 0:KF * D].rearrange("p (k n) -> p k n", k=KF)
                for t in range(NT):
                    for half in range(2):
                        name = f"acc{2 * t + half}"
                        o = fill(l, name)
                        for kc in range(KF):
                            m = pe.matmul(o[:, :], hT[:, (2 * t + kc) * P:(2 * t + kc + 1) * P],
                                          wd[:, kc, half * 512:(half + 1) * 512],
                                          start=kc == 0, stop=kc == KF - 1, skip_group_check=True)
                        filled(l, name, m)

            def run(ps, base, round_):
                n0 = base
                if round_ is None:
                    pe.wait_ge(*read_at(layer[0], "sh0"))
                pe.wait_ge(ps.sel_rd, n0 + 1)
                gather(ps, n0, 0, [])
                if round_ is None:
                    shared_turn(layer[0])
                gather(ps, n0, 1, [(ps.g_sb, 2 * n0 + 1)])
                if round_ is None:
                    shared_down(layer[0])
                turn_sel(ps, n0, 0)

                def body(n, q, b, first, last):
                    pe.wait_ge(ps.g_sb, 2 * n + 2)
                    pe.wait_ge(ps.w_in[0][b], (n - b) * 16 + 32)
                    if not first:
                        pe.wait_ge(ps.hT_sb, n)
                    for k in range(KD):
                        for a in range(2):
                            m = pe.matmul(H[64 * a:64 * a + 64, :], xg[:, k, 64 * a:64 * a + 64],
                                          gu[:, b, a, :, k, :], start=k == 0, stop=k == KD - 1)
                    m.then_inc(ps.h_full, 1)
                    if not last:
                        pe.wait_ge(ps.sel_rd, n + 2)
                        gather(ps, n + 1, 0, [(ps.selT_sb, n + 1)])
                    if not first:
                        combine(ps, n - 1, 1 - b)
                    pe.wait_ge(ps.h_rd, n + 1)
                    for kc in range(KF):
                        m = pe.transpose(H[:, kc * P:(kc + 1) * P], hh[:, 0, kc::KF], ident)
                    m.then_inc(ps.hT_ps, 1)
                    if not last:
                        gather(ps, n + 1, 1, [(ps.g_sb, 2 * n + 3)])
                    pe.wait_ge(ps.w_in[1][b], (n - b) * 8 + 16)
                    pe.wait_ge(ps.hT_sb, n + 1)
                    for half in range(2):
                        if not first:
                            pe.wait_ge(ps.res_rd, 2 * n - 1 + half)
                        for kc in range(KF):
                            for a in range(2):
                                m = pe.matmul(Y[half][64 * a:64 * a + 64, :],
                                              hT[:, kc * P + 64 * a:kc * P + 64 * a + 64],
                                              dn[:, b, a, kc, half * 512:(half + 1) * 512],
                                              start=kc == 0, stop=kc == KF - 1)
                        m.then_inc(ps.y_full, 1)
                    if not last:
                        turn_sel(ps, n + 1, q + 1)
                pairs_of_pass(pe, base, body)
                combine(ps, base + PAIRS - 1, 1)

            def skipped(n):
                for s_, k in ((more.g_full, 2), (more.selT_ps, 1), (more.h_full, 1), (more.hT_ps, 1),
                              (more.y_full, 2), (more.comb, 1)):
                    pe.sem_inc(s_, n * k)

            with pe.Fori(0, DEPTH) as l:
                layer[0] = l
                def mem_here(t):
                    chunk_wait(l, 1)
                    return []
                transposes(l, "memT", mem_sb, mem_here)
                chunk_wait(l, 0)
                for g in range(4):
                    pe.wait_ge(*read_at(l, f"memT{g}"))
                W = [stage[:, h, :].rearrange("p (k n) -> p k n", k=KD) for h in range(2)]
                o = fill(l, "kmT")
                for j in range(2):
                    for k in range(KD):
                        m = pe.matmul(o[:, j * S:(j + 1) * S], W[0][:, k, j * P:(j + 1) * P], memT[:, k, :],
                                      start=k == 0, stop=k == KD - 1)
                filled(l, "kmT", m)
                o = fill(l, "vm")
                for t in range(2):
                    for k in range(KD):
                        m = pe.matmul(o[:, t * 256:(t + 1) * 256], memT[:, k, t * P:(t + 1) * P], W[0][:, k, 256:512],
                                      start=k == 0, stop=k == KD - 1)
                filled(l, "vm", m)
                transposes(l, "xTa", xs, lambda t: [x_before(l)] if t == 0 else [])
                for g in range(4):
                    pe.wait_ge(*read_at(l, f"xTa{g}"))

                def rotate(i):
                    o = fill(l, f"rot{i}")
                    pe.wait_ge(*read_at(l, f"raw{i}"))
                    filled(l, f"rot{i}", pe.matmul(o[:, :], cc("rot"), raw[:, i % 2, :], start=True, stop=True))

                for i in range(4):
                    c = 2 + i // 2
                    if i % 2 == 0:
                        chunk_wait(l, c)
                    o = fill(l, f"raw{i}")
                    for j in range(2):
                        for k in range(KD):
                            m = pe.matmul(o[:, j * S:(j + 1) * S], W[c % 2][:, k, (2 * (i % 2) + j) * P:(2 * (i % 2) + j + 1) * P],
                                          xT[:, k, :], start=k == 0, stop=k == KD - 1)
                    filled(l, f"raw{i}", m)
                    if i:
                        rotate(i - 1)
                chunk_wait(l, 4)
                for t in range(NT):
                    o = fill(l, f"v{t}")
                    for k in range(KD):
                        m = pe.matmul(o[:, :], xT[:, k, t * P:(t + 1) * P], W[0][:, k, :],
                                      start=k == 0, stop=k == KD - 1)
                    filled(l, f"v{t}", m)
                    if t == 0:
                        rotate(3)

                def pool_inputs(t):
                    if t == 0:
                        chunk_wait(l, 5)
                        fill(l, "u")
                    o = bank[BANK_OF["u"]]
                    for k in range(KD):
                        m = pe.matmul(o[:, t * 256:(t + 1) * 256], xT[:, k, t * P:(t + 1) * P], W[1][:, k, 0:256],
                                      start=k == 0, stop=k == KD - 1)
                    if t == NT - 1:
                        filled(l, "u", m)

                def memory_queries(j):
                    if j == 0:
                        fill(l, "qm")
                    o = bank[BANK_OF["qm"]]
                    for k in range(KD):
                        m = pe.matmul(o[:, j * S:(j + 1) * S], W[1][:, k, 256 + j * P:256 + (j + 1) * P], xT[:, k, :],
                                      start=k == 0, stop=k == KD - 1)
                    if j == 1:
                        filled(l, "qm", m)

                def pool_tokens():
                    pe.wait_ge(*read_at(l, "u"))
                    pe.wait_ge(pool_in, 16 * l + 16)
                    o = fill(l, "pooled")
                    for g in range(4):
                        h0 = 64 * (g % 2)
                        for t in range(NT):
                            m = pe.matmul(o[h0:h0 + 64, (g // 2) * S:(g // 2 + 1) * S], uu[:, t, 64 * g:64 * g + 64],
                                          pool_sb[:, t, g, :], start=t == 0, stop=t == NT - 1)
                    filled(l, "pooled", m)

                def pool_channels():
                    pe.wait_ge(*read_at(l, "pooled"))
                    pe.wait_ge(small_in, 80 * l + 80)
                    o = fill(l, "pmix")
                    stand_alone(pe)
                    for g in range(4):
                        h0 = 64 * (g % 2)
                        m = pe.matmul(o[h0:h0 + 64, (g // 2) * S:(g // 2 + 1) * S], wp[h0:h0 + 64, g // 2, :],
                                      pooledT[h0:h0 + 64, g // 2, :], start=True, stop=True)
                    filled(l, "pmix", m)

                def project(i, ks):
                    name, t, half = f"wo{i}", i // 2, i % 2
                    if ks[0] == 0:
                        chunk_wait(l, 6 + half)
                        fill(l, name)
                    o = bank[BANK_OF[name]]
                    for k in ks:
                        pe.wait_ge(*read_at(l, "pmix" if k < 2 else f"o{k - 2}"))
                        m = pe.matmul(o[:, :], mixT[:, k, t * P:(t + 1) * P], W[half][:, k, :],
                                      start=k == 0, stop=k == KD - 1, skip_group_check=True)
                    if ks[-1] == KD - 1:
                        filled(l, name, m)
                beside = {0: [(pool_inputs, 0)], 1: [(pool_inputs, 1)], 2: [(memory_queries, 0)],
                          3: [(memory_queries, 1)], 4: [(pool_tokens,)], 5: [(pool_channels,)],
                          6: [(project, 0, [0, 1, 2, 3])], 7: [(project, 1, [0, 1, 2, 3])],
                          9: [(project, 0, [4, 5]), (project, 1, [4])], 10: [(project, 1, [5])]}
                pe.wait_ge(qk_sb, 4 * l + 4)
                for name in ("v0", "v1", "kmT", "vm"):
                    pe.wait_ge(*read_at(l, name))

                def scores(u):
                    h0, c = 64 * (u % 2), u // 2
                    if u == DSA_HEADS:
                        pe.wait_ge(*read_at(l, "qm"))
                    o = fill(l, f"s{u}")
                    if u < DSA_HEADS:
                        q, k = qkT[h0:h0 + 64, c, :], qkT[h0:h0 + 64, 4 + c, :]
                        pe.matmul(o[:, 0:P], q[:, 0:P], k[:, 0:P], start=True, stop=True)
                        m = pe.matmul(o[:, P:3 * P], q[:, P:S], k, start=True, stop=True)
                    else:
                        c -= 4
                        for t in range(NT):
                            m = pe.matmul(o[:, t * S:(t + 1) * S], qmT[h0:h0 + 64, c, t * P:(t + 1) * P],
                                          kmT[h0:h0 + 64, c, :], start=True, stop=True)
                    filled(l, f"s{u}", m)

                def turn_probs(u):
                    o = fill(l, f"pT{u}")
                    pe.wait_ge(p_rd, UNITS * l + u + 1)
                    src = (0, 1, 2) if u < DSA_HEADS else (0, 2, 1, 3)
                    for j, s_ in enumerate(src):
                        m = pe.transpose(o[:, j * P:(j + 1) * P], prob[:, u % 2, s_ * P:(s_ + 1) * P], ident)
                    filled(l, f"pT{u}", m)

                def outputs(u):
                    h0 = 64 * (u % 2)
                    o = bank[BANK_OF[f"o{u // 2}"]]
                    if u % 2 == 0:
                        fill(l, f"o{u // 2}")
                    pe.wait_ge(*read_at(l, f"pT{u}"))
                    pt = pT[:, u % 2, :]
                    if u < DSA_HEADS:
                        pe.matmul(o[h0:h0 + 64, 0:S], vv[:, 0, 64 * u:64 * u + 64], pt[:, 0:S], start=True, stop=False)
                        m = pe.matmul(o[h0:h0 + 64, P:S], vv[:, 1, 64 * u:64 * u + 64], pt[:, S:S + P], start=False, stop=True)
                    else:
                        h = u - DSA_HEADS
                        for t in range(2):
                            m = pe.matmul(o[h0:h0 + 64, 0:S], vm[:, t, 64 * h:64 * h + 64], pt[:, t * S:(t + 1) * S],
                                          start=t == 0, stop=t == 1)
                    if u % 2:
                        filled(l, f"o{u // 2}", m)
                scores(0)
                for u in range(UNITS + 1):
                    if u + 1 < UNITS:
                        scores(u + 1)
                    for what, *args in beside.get(u, []):
                        what(*args)
                    if u < UNITS:
                        turn_probs(u)
                    if u:
                        outputs(u - 1)
                project(0, [6, 7])
                project(1, [6, 7])
                project(2, list(range(KD)))
                project(3, list(range(KD)))
                transposes(l, "xTb", xs, lambda t: [x_at(l, 0, t)])
                for g in range(4):
                    pe.wait_ge(*read_at(l, f"xTb{g}"))
                o = fill(l, "logit")
                for t in range(NT):
                    for k in range(KD):
                        m = pe.matmul(o[:, t * E:(t + 1) * E], xT[:, k, t * P:(t + 1) * P], wr[:, k, :],
                                      start=k == 0, stop=k == KD - 1)
                filled(l, "logit", m)

                def shared_up(t):
                    o = fill(l, f"sh{t}")
                    for k in range(KD):
                        m = pe.matmul(o[:, :], xT[:, k, t * P:(t + 1) * P], W[0][:, k, :],
                                      start=k == 0, stop=k == KD - 1)
                    filled(l, f"sh{t}", m)
                chunk_wait(l, 8)
                shared_up(0)
                o = fill(l, "cum")
                pe.wait_ge(chosen_rd, l + 1)
                ch = [chosenb[:, t * E:(t + 1) * E] for t in range(NT)]
                pe.matmul(o[:, 0:E], beforeb[:], ch[0], start=True, stop=True)
                pe.matmul(o[:, E:2 * E], onesb[:], ch[0], start=True, stop=False)
                pe.matmul(o[:, E:2 * E], beforeb[:], ch[1], start=False, stop=True)
                pe.matmul(o[:, 2 * E:3 * E], onesb[:], ch[0], start=True, stop=False)
                filled(l, "cum", pe.matmul(o[:, 2 * E:3 * E], onesb[:], ch[1], start=False, stop=True))
                shared_up(1)
                pe.wait_ge(split_rd, 2 * l + 2)
                pe.wait_ge(route_rd, l + 1)
                passes(pe, l, run, skipped)

        @block.scalar
        def _(act):
            act.wait_ge(setup_done, 1)
            def copy(out_, in_, **kw):
                return act.activation(out_, in_, ACT.Copy, **kw)

            def take(l, name):
                act.wait_ge(*full_at(l, name))
                return bank[BANK_OF[name]]

            def evac(l, name, dst):
                copy(dst, take(l, name)[:, :]).then_inc(read[BANK_OF[name]], 1)

            def run(ps, base, round_):
                def g_half(n, half):
                    act.wait_ge(ps.g_full, 2 * n + half + 1)
                    copy(xg[:, 4 * half:4 * half + 4, :].rearrange("p k c -> p (k c)"), G[:, :]).then_inc(ps.g_sb, 1)
                g_half(base, 0)
                g_half(base, 1)

                def body(n, q, b, first, last):
                    act.wait_ge(ps.h_full, n + 1)
                    act.activation(sg[:, 0, :], H[:, 0:F], ACT.Silu).then_inc(ps.silu_rd, 1)
                    if not last:
                        g_half(n + 1, 0)
                        g_half(n + 1, 1)
                    act.wait_ge(ps.selT_sb, n + 1)
                    for half in range(2):
                        act.wait_ge(ps.y_full, 2 * n + half + 1)
                        copy(ysp[:, 0, half * 512:(half + 1) * 512], Y[half][:, :], scale=wslot[:, b:b + 1])\
                            .then_inc(ps.hi_rd, 1)
                    for half in range(2):
                        act.wait_ge(ps.res_rd, 2 * n + half + 1)
                        copy(ysp[:, 1, half * 512:(half + 1) * 512], yres[:, half * 512:(half + 1) * 512])\
                            .then_inc(ps.mid_rd, 1)
                pairs_of_pass(act, base, body)

            def skipped(n):
                for s_, k in ((more.g_sb, 2), (more.silu_rd, 1), (more.hi_rd, 2), (more.mid_rd, 2)):
                    act.sem_inc(s_, n * k)

            with act.Fori(0, DEPTH) as l:
                for g in range(4):
                    evac(l, f"memT{g}", memT[:, 2 * g:2 * g + 2, :].rearrange("p k s -> p (k s)"))
                evac(l, "kmT", kmT.rearrange("p k s -> p (k s)"))
                evac(l, "vm", vm.rearrange("p k s -> p (k s)"))
                for g in (0, 2):
                    evac(l, f"xTa{g}", xT[:, 2 * g:2 * g + 2, :].rearrange("p k s -> p (k s)"))
                for i in range(4):
                    if i >= 2:
                        act.wait_ge(qk_sb, 4 * l + i - 1)
                    evac(l, f"raw{i}", raw[:, i % 2, :])
                evac(l, "v0", vv[:, 0, :])
                evac(l, "v1", vv[:, 1, :])

                def exps(u):
                    act.wait_ge(negm_rd, UNITS * l + u + 1)
                    if u < DSA_HEADS:
                        for t, a, z in ((0, 0, P), (1, P, 3 * P)):
                            m = act.activation(prob[:, u % 2, a:z], prob[:, u % 2, a:z], ACT.Exp,
                                               bias=negm[u % 2][:, t:t + 1], scale=SCALE)
                        m.then_inc(exp_rd, 1)
                    else:
                        if u >= 2:
                            act.wait_ge(*full_at(l, f"pT{u - 2}"))
                        s_ = take(l, f"s{u}")
                        for t in range(NT):
                            m = act.activation(prob[:, u % 2, t * S:(t + 1) * S], s_[:, t * S:(t + 1) * S], ACT.Exp,
                                               bias=negm[u % 2][:, t:t + 1], scale=SCALE,
                                               accum_out=den[u % 2][:, t:t + 1])
                        m.then_inc(read[BANK_OF[f"s{u}"]], 1)

                def turned(u):
                    w = 3 * P if u < DSA_HEADS else 4 * P
                    if u >= 2:
                        act.wait_ge(*full_at(l, f"o{(u - 2) // 2}"))
                    s_ = take(l, f"pT{u}")
                    copy(pT[:, u % 2, 0:w], s_[:, 0:w]).then_inc(read[BANK_OF[f"pT{u}"]], 1)
                for u in range(UNITS):
                    exps(u)
                    if u:
                        turned(u - 1)
                    if u == 2:
                        evac(l, "u", uu.rearrange("p t n -> p (t n)"))
                    if u == 4:
                        evac(l, "qm", qmT.rearrange("p k s -> p (k s)"))
                turned(UNITS - 1)

                def sqrt(i, t):
                    act.wait_ge(var_rd, 4 * l + 2 * i + t + 1)
                    act.activation(std[:, t:t + 1], mv[:, t, 1:2], ACT.Sqrt, bias=epst[:, 0:1]).then_inc(std_rd, 1)

                def split(t, part):
                    if part == 0:
                        act.wait_ge(*x_at(l, 0, t))
                        copy(xsp[:, t, 0, :], xs[:, t, :]).then_inc(split_hi, 1)
                    else:
                        act.wait_ge(split_rs, 2 * l + t + 1)
                        copy(xsp[:, t, 1, :], xres[:, t, :]).then_inc(split_hi, 1)
                sqrt(0, 0)
                split(0, 0)
                sqrt(0, 1)
                for g in (0, 2):
                    evac(l, f"xTb{g}", xT[:, 2 * g:2 * g + 2, :].rearrange("p k s -> p (k s)"))
                act.activation(sig, take(l, "logit")[:, 0:NT * E], ACT.Exp, scale=-1.0)\
                    .then_inc(read[BANK_OF["logit"]], 1)
                split(1, 0)
                split(0, 1)
                split(1, 1)
                for t in range(NT):
                    act.wait_ge(*full_at(l, f"sh{t}"))
                    act.activation(sg[:, t, :], bank[BANK_OF[f"sh{t}"]][:, 0:F], ACT.Silu).then_inc(ssilu, 1)
                passes(act, l, run, skipped)
                for t in range(NT):
                    sqrt(1, t)

        @block.vector
        def _(dve):
            dve.memset(onesb[:], 1.0)
            dve.memset(epst[:], EPS)
            dve.memset(small[:], 0.0)
            dve.wait_ge(const_in, 16)
            dve.tensor_copy(identb[:], ident)
            dve.tensor_copy(beforeb[:], cc("before")).then_inc(setup_done, 1)
            for s_ in [*read, x_ready]:
                dve.sem_inc(s_, 1)
            dve.wait_ge(x_in, 16)
            links = [0]
            layer = [None]

            def link(ins):
                links[0] += 1
                ins.then_inc(dve_link, 1)
                dve.wait_ge(dve_link, layer[0] * DVE_LINKS + links[0])

            def take(l, name):
                dve.wait_ge(*full_at(l, name))
                return bank[BANK_OF[name]]

            def evac(l, name, dst):
                dve.tensor_copy(dst, take(l, name)[:, :]).then_inc(read[BANK_OF[name]], 1)

            def residual_stats(l, i, t, names):
                for h in range(2):
                    v = xs[:, t, h * 512:(h + 1) * 512]
                    dve.scalar_tensor_tensor(v, v, ALPHA, take(l, names[h])[:, :], ALU.mult, ALU.add)\
                        .then_inc(read[BANK_OF[names[h]]], 1)
                for h in range(2):
                    dve.wait_ge(*read_at(l, names[h]))
                    m = dve.bn_stats(stats[:, t, h, :], xs[:, t, h * 512:(h + 1) * 512])
                link(m)
                stand_alone(dve)
                dve.bn_aggr(mv[:, t, :], stats[:, t, :, :]).then_inc(var_rd, 1)

            def normalised(l, i, t):
                dve.wait_ge(std_rd, 4 * l + 2 * i + t + 1)
                dve.reciprocal(rstd[:, t:t + 1], std[:, t:t + 1])
                dve.wait_ge(ln_in, 64 * l + 32 * i + 32)
                v = xs[:, t, :]
                link(dve.scalar_tensor_tensor(v, v, mv[:, t, 0:1], lng, ALU.subtract, ALU.mult))
                dve.scalar_tensor_tensor(v, v, rstd[:, t:t + 1], lnb, ALU.mult, ALU.add).then_inc(x_ready, 1)

            def split_residual(l, t):
                dve.wait_ge(split_hi, 4 * l + t + 1)
                dve.tensor_tensor(xres[:, t, :], xs[:, t, :], xsp[:, t, 0, :], ALU.subtract).then_inc(split_rs, 1)

            def split_last(l, t):
                dve.wait_ge(split_hi, 4 * l + 2 + t + 1)
                dve.tensor_tensor(xsp[:, t, 2, :], xres[:, t, :], xsp[:, t, 1, :], ALU.subtract).then_inc(split_rd, 1)

            def run(ps, base, round_):
                if round_ is not None:
                    dve.tensor_scalar(pos, pos, -float(SLOTS), None, ALU.add).then_inc(pos_rd, 1)
                    dve.wait_ge(pos_rd, round_ + 1)
                slots = cc("slot").unsqueeze(1).to_broadcast([P, 2, SLOTS])
                posv = pos.rearrange("p (t r e) -> p t r e", t=NT, e=2)

                def build_sel(n, q, wait):
                    if wait:
                        dve.wait_ge(ps.selT_ps, n)
                    for t in range(NT):
                        m = dve.tensor_tensor(sel[:, t, :].rearrange("p (e c) -> p e c", e=2), slots,
                                              posv[:, t, q, :].unsqueeze(2).to_broadcast([P, 2, SLOTS]), ALU.is_equal)
                    m.then_inc(ps.sel_rd, 1)

                def take_selT(n, b):
                    dve.wait_ge(ps.selT_ps, n + 1)
                    dve.tensor_copy(selT[:, b, :], G[:].bitcast(BF16)[:, 0:S])
                    for e in range(2):
                        m = dve.tensor_reduce(wslot[64 * e:64 * e + 64, b:b + 1], G[64 * e:64 * e + 64, 256 + 3 * e:259 + 3 * e],
                                              AX.X, ALU.add)
                    m.then_inc(ps.selT_sb, 1)
                build_sel(base, 0, False)
                if round_ is None:
                    l = layer[0]
                    for t in range(NT):
                        dve.wait_ge(ssilu, 2 * l + t + 1)
                        name = f"sh{t}"
                        dve.tensor_tensor(hh[:, t, :], sg[:, t, :], take(l, name)[:, F:2 * F], ALU.mult)\
                            .then_inc(read[BANK_OF[name]], 1)
                    evac(l, "shT", hT)
                take_selT(base, 0)

                def body(n, q, b, first, last):
                    if not last:
                        build_sel(n + 1, q + 1, True)
                    dve.wait_ge(ps.silu_rd, n + 1)
                    dve.tensor_tensor(hh[:, 0, :], sg[:, 0, :], H[:, F:2 * F], ALU.mult).then_inc(ps.h_rd, 1)
                    dve.wait_ge(ps.hT_ps, n + 1)
                    dve.tensor_copy(hT[:, 0:F], H[:, 0:F]).then_inc(ps.hT_sb, 1)
                    dve.wait_ge(ps.selT_sb, n + 1)
                    if not first:
                        dve.wait_ge(ps.lo_rd, 2 * n)
                    for half in range(2):
                        dve.wait_ge(ps.hi_rd, 2 * n + half + 1)
                        dve.scalar_tensor_tensor(yres[:, half * 512:(half + 1) * 512], Y[half][:, :], wslot[:, b:b + 1],
                                                 ysp[:, 0, half * 512:(half + 1) * 512], ALU.mult, ALU.subtract)\
                            .then_inc(ps.res_rd, 1)
                    if not last:
                        take_selT(n + 1, 1 - b)
                    for half in range(2):
                        dve.wait_ge(ps.mid_rd, 2 * n + half + 1)
                        dve.tensor_tensor(ysp[:, 2, half * 512:(half + 1) * 512], yres[:, half * 512:(half + 1) * 512],
                                          ysp[:, 1, half * 512:(half + 1) * 512], ALU.subtract).then_inc(ps.lo_rd, 1)
                pairs_of_pass(dve, base, body)
                dve.wait_ge(ps.comb, base + PAIRS)

            def skipped(n):
                for s_, k in ((more.sel_rd, 1), (more.selT_sb, 1), (more.h_rd, 1), (more.hT_sb, 1),
                              (more.res_rd, 2), (more.lo_rd, 2)):
                    dve.sem_inc(s_, n * k)
                dve.sem_inc(pos_rd, n // PAIRS)

            with dve.Fori(0, DEPTH) as l:
                layer[0] = l
                links[0] = 0
                for g in (1, 3):
                    evac(l, f"xTa{g}", xT[:, 2 * g:2 * g + 2, :].rearrange("p k s -> p (k s)"))
                cos2 = cc("cos").unsqueeze(1).to_broadcast([P, 2, S])
                sin2 = cc("sin").unsqueeze(1).to_broadcast([P, 2, S])
                for i in range(4):
                    dve.wait_ge(*read_at(l, f"raw{i}"))
                    dst = qkT[:, 2 * i:2 * i + 2, :]
                    dve.tensor_tensor(dst, raw[:, i % 2, :].rearrange("p (c s) -> p c s", s=S), cos2, ALU.mult)
                    r_ = take(l, f"rot{i}")
                    if i:
                        dve.wait_ge(qk_sb, 4 * l + i)
                    m = dve.tensor_tensor(rt.rearrange("p (c s) -> p c s", s=S), r_[:, :].rearrange("p (c s) -> p c s", s=S),
                                          sin2, ALU.mult)
                    m.then_inc(read[BANK_OF[f"rot{i}"]], 1)
                    dve.wait_ge(*read_at(l, f"rot{i}"))
                    dve.tensor_tensor(dst, dst, rt.rearrange("p (c s) -> p c s", s=S), ALU.add).then_inc(qk_sb, 1)

                def pool_scaled():
                    dve.wait_ge(small_in, 80 * l + 80)
                    o = take(l, "pmix")
                    for j in range(2):
                        m = dve.tensor_scalar(mixT[:, j, :], o[:, j * S:(j + 1) * S], psc[:, j:j + 1], None, ALU.mult)
                    m.then_inc(read[BANK_OF["pmix"]], 1)

                def maxima(u):
                    i = u % 2
                    o = take(l, f"s{u}")
                    if u < DSA_HEADS:
                        if u >= 2:
                            dve.wait_ge(*full_at(l, f"pT{u - 2}"))
                        stand_alone(dve)
                        for t, a, z in ((0, 0, P), (1, P, 3 * P)):
                            m = dve.tensor_tensor_reduce(prob[:, i, a:z], o[:, a:z], cc("bias")[:, a:z], 1.0, -3e38,
                                                         ALU.add, ALU.max, mx[i][:, t:t + 1])
                        m.then_inc(read[BANK_OF[f"s{u}"]], 1)
                        dve.wait_ge(*read_at(l, f"s{u}"))
                    else:
                        link(dve.tensor_reduce(mx[i], o[:, :].rearrange("p (t s) -> p t s", t=NT), AX.X, ALU.max))
                    dve.tensor_scalar(negm[i], mx[i], -SCALE, None, ALU.mult).then_inc(negm_rd, 1)

                def normalise(u):
                    i = u % 2
                    if u < DSA_HEADS:
                        dve.wait_ge(exp_rd, DSA_HEADS * l + u + 1)
                    else:
                        dve.wait_ge(*read_at(l, f"s{u}"))
                    cuts = ((0, 0, P), (1, P, 3 * P)) if u < DSA_HEADS else ((0, 0, S), (1, S, 2 * S))
                    if u < DSA_HEADS:
                        for t, a, z in cuts:
                            m = dve.tensor_tensor_reduce(prob[:, i, a:z], prob[:, i, a:z], cc("mult")[:, a:z], 1.0, 0.0,
                                                         ALU.mult, ALU.add, den[i][:, t:t + 1])
                        link(m)
                    link(dve.reciprocal(rden[i], den[i]))
                    for t, a, z in cuts:
                        m = dve.tensor_scalar(prob[:, i, a:z], prob[:, i, a:z], rden[i][:, t:t + 1], None, ALU.mult)
                    m.then_inc(p_rd, 1)

                def heads_out(c):
                    name = f"o{c}"
                    m = dve.tensor_copy(mixT[:, 2 + c, :], take(l, name)[:, 0:S])
                    m.then_inc(read[BANK_OF[name]], 1)
                maxima(0)
                for u in range(UNITS):
                    if u + 1 < UNITS:
                        maxima(u + 1)
                    normalise(u)
                    if u >= 3 and u % 2:
                        heads_out((u - 3) // 2)
                    if u == 4:
                        evac(l, "pooled", pooledT.rearrange("p k s -> p (k s)"))
                    if u == 5:
                        pool_scaled()
                heads_out(UNITS // 2 - 1)
                residual_stats(l, 0, 0, ("wo0", "wo1"))
                normalised(l, 0, 0)
                split_residual(l, 0)
                residual_stats(l, 0, 1, ("wo2", "wo3"))
                normalised(l, 0, 1)

                for g in (1, 3):
                    evac(l, f"xTb{g}", xT[:, 2 * g:2 * g + 2, :].rearrange("p k s -> p (k s)"))
                split_residual(l, 1)
                split_last(l, 0)
                dve.wait_ge(*read_at(l, "logit"))
                link(dve.tensor_scalar(sig, sig, 1.0, None, ALU.add))
                link(dve.reciprocal(sig, sig))
                link(dve.tensor_tensor(biased.rearrange("p (t e) -> p t e", t=NT), sig.rearrange("p (t e) -> p t e", t=NT),
                                       rb[:].unsqueeze(1).to_broadcast([P, NT, E]), ALU.add))
                stand_alone(dve)
                for j in range(NT * GROUPS):
                    m = dve.max(g8[:, 8 * j:8 * j + 8], biased[:, 8 * j:8 * j + 8])
                link(m)
                g8v = g8.rearrange("p (j k) -> p j k", k=8)
                link(dve.tensor_tensor(gs, g8v[:, :, 0], g8v[:, :, 1], ALU.add))
                for t in range(NT):
                    v = gs[:, t * GROUPS:(t + 1) * GROUPS]
                    other = v.unsqueeze(1).to_broadcast([P, GROUPS, GROUPS])
                    own = v.unsqueeze(2).to_broadcast([P, GROUPS, GROUPS])
                    c1 = cmp1.rearrange("p (i j) -> p i j", j=GROUPS)
                    c2 = cmp2.rearrange("p (i j) -> p i j", j=GROUPS)
                    dve.tensor_tensor(c1, other, own, ALU.is_gt)
                    link(dve.tensor_tensor(c2, other, own, ALU.is_equal))
                    link(dve.tensor_tensor(cmp2, cmp2, cc("tri"), ALU.mult))
                    link(dve.tensor_tensor(cmp1, cmp1, cmp2, ALU.add))
                    link(dve.tensor_reduce(rank[:, t * GROUPS:(t + 1) * GROUPS], c1, AX.X, ALU.add))
                link(dve.tensor_scalar(rank, rank, float(TOP_GROUPS), None, ALU.is_lt))
                link(dve.tensor_scalar(gneg, rank, BIG, -BIG, ALU.mult, ALU.add))
                b3 = biased.rearrange("p (j k) -> p j k", k=8)
                m3 = masked.rearrange("p (j k) -> p j k", k=8)
                link(dve.tensor_tensor(m3, b3, rank.unsqueeze(2).to_broadcast([P, NT * GROUPS, 8]), ALU.mult))
                link(dve.tensor_tensor(m3, m3, gneg.unsqueeze(2).to_broadcast([P, NT * GROUPS, 8]), ALU.add))
                stand_alone(dve)
                for t in range(NT):
                    m = dve.max(top[:, 8 * t:8 * t + 8], masked[:, t * E:(t + 1) * E])
                link(m)
                stand_alone(dve)
                for t in range(NT):
                    m = dve.match_replace(chosen[:, t * E:(t + 1) * E], top[:, 8 * t:8 * t + 8],
                                          masked[:, t * E:(t + 1) * E], GONE)
                link(m)
                link(dve.tensor_scalar(chosen, chosen, GONE / 2, None, ALU.is_lt))
                dve.tensor_copy(chosenb, chosen).then_inc(chosen_rd, 1)
                for t in range(NT):
                    m = dve.tensor_tensor_reduce(wts[:, t * E:(t + 1) * E], chosen[:, t * E:(t + 1) * E],
                                                 sig[:, t * E:(t + 1) * E], 1.0, 0.0, ALU.mult, ALU.add, wsum[:, t:t + 1])
                link(m)
                link(dve.reciprocal(wrec, wsum))
                for t in range(NT):
                    m = dve.tensor_scalar(wts[:, t * E:(t + 1) * E], wts[:, t * E:(t + 1) * E], wrec[:, t:t + 1],
                                          ROUTED_SCALE, ALU.mult, ALU.mult)
                link(m)
                wp_ = [w3[:, :, :, s_] for s_ in range(3)]
                wv = wts.rearrange("p (t e) -> p t e", t=NT)
                wrv = wres.rearrange("p (t e) -> p t e", t=NT)
                link(dve.tensor_copy(wp_[0], wv))
                link(dve.tensor_tensor(wrv, wv, wp_[0], ALU.subtract))
                link(dve.tensor_copy(wp_[1], wrv))
                dve.tensor_tensor(wp_[2], wrv, wp_[1], ALU.subtract)
                o = take(l, "cum")
                link(dve.scalar_tensor_tensor(pos, o[:, 0:NT * E], 1.0, chosen, ALU.add, ALU.mult))
                dve.tensor_scalar(pos, pos, -1.0, None, ALU.add)
                m = dve.tensor_reduce(cntf, o[:, NT * E:(NT + 1) * E], AX.X, ALU.max)
                m.then_inc(read[BANK_OF["cum"]], 1)
                dve.wait_ge(*read_at(l, "cum"))
                dve.tensor_copy(counts_i[:], cntf).then_inc(route_rd, 1)
                split_last(l, 1)
                passes(dve, l, run, skipped)
                for t in range(NT):
                    residual_stats(l, 1, t, (f"acc{2 * t}", f"acc{2 * t + 1}"))
                for t in range(NT):
                    normalised(l, 1, t)
                assert links[0] == DVE_LINKS, links[0]


_INS = ["x", "mem", "w_in", "w_pool", "pool_scale", "w_mem_kv", "w_out", "ln1_g", "ln1_b", "w_router",
        "router_bias", "w_gate", "w_up", "w_down", "ws_gate", "ws_up", "ws_down", "ln2_g", "ln2_b"]


def kernel(**inputs):
    import concourse.bacc as bacc
    from concourse.bass_utils import run_bass_kernel_spmd

    nc = bacc.Bacc("TRN2", target_bir_lowering=False, num_devices=1)
    consts, pool_mat = constants()
    given = {n: np.ascontiguousarray(inputs[n]) for n in _INS}
    given["consts"], given["pool_mat"] = consts, pool_mat
    arrays, args = {}, []
    for name, a in given.items():
        arrays[f"in_{name}"] = a
        args.append(nc.dram_tensor(f"in_{name}", a.shape, mybir.dt.from_np(a.dtype), kind="ExternalInput").ap())
    args.append(nc.dram_tensor("out_x", (1, S, D), F32, kind="ExternalOutput").ap())
    build(nc, *args)
    r = run_bass_kernel_spmd(nc, [arrays], core_ids=[0])
    return r.results[0]["out_x"]
```

```python
from contextlib import ExitStack

import numpy as np
import concourse.bass as bass
from concourse import mybir

F32 = mybir.dt.float32
BF16 = mybir.dt.bfloat16
I32 = mybir.dt.int32
ALU = mybir.AluOpType
ACT = mybir.ActivationFunctionType
AX = mybir.AxisListType

P = 128
DEPTH, D, S = 2, 1024, 256
NT = S // P
KD = D // P
HD = 64
DSA_HEADS, MEM_HEADS = 8, 4
SCALE = HD ** -0.5
WINDOWS = (2, 4, 8, 16)
PATTERNS = ((128, 1), (512, 4), (2048, 16))
ROT = HD // 4
POOL_W = D // 4
E, TOPK, GROUPS, TOP_GROUPS = 64, 8, 8, 4
F = 256
KF = F // P
SLOTS = 64
PAIRS = E // 2
PAIR_STEP = 6
PEELED = PAIRS % PAIR_STEP
USES = [len(range(g, PAIRS, 3)) for g in range(3)]
ROUNDS = S // SLOTS
ROUTED_SCALE = 2.5
ALPHA = float((2 * DEPTH) ** 0.25)
EPS = 1e-5
BIG = 1e30
GONE = -3e38

CONSTS = {}
_at = 0
for _n, _w in (("ident", P), ("rot", P), ("before", P), ("slot", SLOTS), ("tri", GROUPS * GROUPS),
               ("cos", S), ("sin", S), ("bias", 3 * P), ("mult", 3 * P)):
    CONSTS[_n] = (_at, _at + _w)
    _at += _w
NCONST = _at


def constants():
    c = np.zeros((P, NCONST), np.float32)

    def put(name, v):
        c[:, CONSTS[name][0]:CONSTS[name][1]] = v
    i, j = np.arange(P)[:, None], np.arange(P)[None]
    put("ident", i == j)
    put("before", i < j)
    put("slot", np.arange(SLOTS)[None])
    g = np.arange(GROUPS)
    put("tri", (g[None, :] < g[:, None]).reshape(1, -1))
    half = ROT // 2
    r = np.zeros((P, P))
    for h in range(0, P, HD):
        for d in range(half):
            r[h + d + half, h + d] = -1
            r[h + d, h + d + half] = 1
    put("rot", r)
    inv = np.float32(500000.0) ** (-np.arange(0, ROT, 2, dtype=np.float32) / np.float32(ROT))
    ang = np.arange(S, dtype=np.float32)[:, None] * inv[None]
    cos, sin = np.ones((P, S)), np.zeros((P, S))
    for h in range(0, P, HD):
        for d in range(ROT):
            cos[h + d] = np.cos(ang[:, d % half])
            sin[h + d] = np.sin(ang[:, d % half])
    put("cos", cos)
    put("sin", sin)
    qi, kj = np.arange(S)[:, None], np.arange(S)[None]
    m = np.zeros((S, S))
    for window, dil in PATTERNS:
        d = qi - kj
        m += (d >= 0) & (d % dil == 0) & (d // dil <= window // dil)
    m = np.concatenate([m[:P, :P], m[P:]], axis=1)
    put("mult", m)
    put("bias", np.where(m > 0, 0.0, -BIG))
    s = np.arange(S)
    pool = np.zeros((S, len(WINDOWS), S), np.float32)
    for n, w in enumerate(WINDOWS):
        inside = (qi <= s[None]) & (qi > s[None] - w)
        pool[:, n] = inside / np.minimum(s + 1, w)[None] - (qi == s[None])
    pool = pool.reshape(NT, P, -1).transpose(1, 0, 2).reshape(P, -1)
    return c, np.ascontiguousarray(pool.astype(np.float32))


UNITS = DSA_HEADS + MEM_HEADS
FILLS = ([(f"memT{g}", 4 + g) for g in range(4)] + [("kmT", 4), ("vm", 5)]
         + [(f"xTa{g}", g) for g in range(4)]
         + [(f"{a}{i}", (2 if a == "raw" else 6) + i % 2) for i in range(4) for a in ("raw", "rot")]
         + [("v0", 0), ("v1", 1)])
for _u in range(UNITS):
    FILLS += [(f"s{_u}", 4 + _u % 2)]
    FILLS += {0: [("u", 2)], 2: [("qm", 3)], 4: [("pooled", 2)], 5: [("pmix", 3)],
              6: [("wo0", 2)], 7: [("wo1", 3)]}.get(_u, [])
    FILLS += [(f"pT{_u}", 6 + _u % 2)]
    if _u % 2:
        FILLS += [(f"o{_u // 2}", (_u // 2) % 2)]
FILLS += [("wo2", 4), ("xTb0", 6), ("xTb1", 7), ("wo3", 5), ("logit0", 2), ("sh0", 4), ("xTb2", 0), ("xTb3", 1)]
FILLS += [("logit1", 3), ("sh1", 5), ("cum", 2), ("shT", 6)]
FILLS += [(f"acc{i}", i) for i in range(4)]
PER_BANK = [sum(b == n for _, b in FILLS) for n in range(8)]
BANK_OF = dict(FILLS)
ORDER = {name: sum(b == bank for _, b in FILLS[:i]) for i, (name, bank) in enumerate(FILLS)}

CHUNKS = ["mem", "kv", "q", "k", "v", "uqm", "wo0", "wo1", "sgu", "sd"]
LAST_USE = ["memT3", "vm", "raw1", "raw3", "v1", "qm", "wo2", "wo3", "sh1", "acc3"]
DVE_LINKS = 77


def build(nc, x, mem, w_in, w_pool, pool_scale, w_mem_kv, w_out, ln1_g, ln1_b, w_router,
          router_bias, w_gate, w_up, w_down, ws_gate, ws_up, ws_down, ln2_g, ln2_b,
          consts, pool_mat, out):
    with ExitStack() as ctx:
        def sb(name, shape, dt=F32):
            return ctx.enter_context(nc.sbuf_tensor(name, shape, dt))

        def sem(name):
            return ctx.enter_context(nc.semaphore(name))

        bank = [ctx.enter_context(nc.psum_tensor(f"bank{i}", [P, 512], F32)) for i in range(8)]
        acc = bank[0:4]
        G, H, Y = bank[4], bank[5], bank[6:8]

        gu = sb("gu", [P, 2, 2, 2, KD, F])
        dn = sb("dn", [P, 2, 2, KF, D])
        stage = sb("stage", [P, 2, KD * 512])
        xs = sb("xs", [P, NT, D])
        xT = sb("xT", [P, KD, S])
        cst = sb("cst", [P, NCONST])
        r8 = sb("r8", [P, 2048])
        small = sb("small", [P, 64])
        identb = sb("identb", [P, P], BF16)
        beforeb = sb("beforeb", [P, P], BF16)
        onesb = sb("onesb", [P, P], BF16)
        wr = sb("wr", [P, KD, E])
        rb = sb("rb", [P, E])
        wp = sb("wp", [P, 2, HD])
        psc = sb("psc", [P, 2])
        epst = sb("epst", [P, 1])
        scratch = sb("scratch", [P, 10752])
        off = [0]

        def part(n, dt=F32):
            v = scratch[:, off[0]:off[0] + n]
            off[0] += n
            assert off[0] <= 10752, off[0]
            return v if dt == F32 else v.bitcast(dt)
        qkT = part(8 * S).rearrange("p (c s) -> p c s", s=S)
        vv = part(NT * 512).rearrange("p (t n) -> p t n", t=NT)
        qmT = part(2 * S).rearrange("p (c s) -> p c s", s=S)
        kmT = part(2 * S).rearrange("p (c s) -> p c s", s=S)
        vm = part(2 * S).rearrange("p (t n) -> p t n", t=2)
        mixT = part(KD * S).rearrange("p (c s) -> p c s", s=S)
        uu = part(NT * 256).rearrange("p (t n) -> p t n", t=NT)
        pooledT = part(2 * S).rearrange("p (c s) -> p c s", s=S)
        raw = part(2 * 512).rearrange("p (b n) -> p b n", b=2)
        rt = part(512)
        pT = part(2 * 512).rearrange("p (b n) -> p b n", b=2)
        memT = mixT
        off[0] = 0
        xsp = part(NT * 3 * D // 2, BF16).rearrange("p (t s d) -> p t s d", t=NT, s=3)
        xres = part(NT * D).rearrange("p (t d) -> p t d", t=NT)
        ysp = part(3 * D // 2, BF16).rearrange("p (s d) -> p s d", s=3)
        xg = part(KD * P).rearrange("p (k c) -> p k c", k=KD)
        hh = part(2 * F).rearrange("p (t n) -> p t n", t=NT)
        hT = part(2 * F)
        sg = part(2 * F).rearrange("p (t n) -> p t n", t=NT)
        sel = part(NT * P // 2, BF16).rearrange("p (t c) -> p t c", t=NT)
        selT = part(2 * S // 2, BF16).rearrange("p (b s) -> p b s", b=2)
        pos = part(NT * E)
        w3 = part(NT * E * 3 // 2, BF16).rearrange("p (t e s) -> p t e s", t=NT, s=3)
        off[0] = NT * 3 * D // 2 + NT * D
        sig = part(NT * E)
        biased = part(NT * E)
        masked = part(NT * E)
        chosen = part(NT * E)
        wts = part(NT * E)
        wres = part(NT * E)
        chosenb = part(NT * E // 2, BF16)
        g8 = part(NT * GROUPS * 8)
        gs = part(NT * GROUPS)
        cmp1 = part(GROUPS * GROUPS)
        cmp2 = part(GROUPS * GROUPS)
        rank = part(NT * GROUPS)
        gneg = part(NT * GROUPS)
        top = part(NT * 8)
        assert off[0] <= NT * 3 * D // 2 + NT * D + 3 * D // 2
        counts_i = sb("counts_i", [P, 1], I32)
        yres = xres[:, 0, :]

        GU = [gu[:, 0], gu[:, 1],
              stage[:].rearrange("p g (e k n) -> p e g k n", e=2, k=KD)]

        def cc(name):
            return cst[:, CONSTS[name][0]:CONSTS[name][1]]
        ident = cc("ident")
        mem_sb = stage[:, 0, 0:2 * D].rearrange("p (t d) -> p t d", t=2)
        pool_sb = r8[:].rearrange("p (t g s) -> p t g s", t=NT, g=len(WINDOWS))
        prob = raw
        lng, lnb = r8[:, 0:D], r8[:, D:2 * D]

        mx = [small[:, 0:2], small[:, 2:4]]
        negm = [small[:, 4:6], small[:, 6:8]]
        den = [small[:, 8:10], small[:, 10:12]]
        rden = [small[:, 12:14], small[:, 14:16]]
        mv = small[:, 16:20].rearrange("p (t n) -> p t n", t=NT)
        std = small[:, 20:22]
        rstd = small[:, 22:24]
        stats = small[:, 24:48].rearrange("p (t h n) -> p t h n", t=NT, h=2)
        wsum = small[:, 48:50]
        wrec = small[:, 50:52]
        wslot = small[:, 52:54]
        cntf = small[:, 54:55]

        full = [sem(f"bank{i}_full") for i in range(8)]
        read = [sem(f"bank{i}_read") for i in range(8)]
        const_in = sem("const_in")
        carried = sem("carried")
        x_in = sem("x_in")
        setup_done = sem("setup_done")
        small_in = sem("small_in")
        pool_in = sem("pool_in")
        ln_in = sem("ln_in")
        chunk_in = [sem(f"chunk_in{i}") for i in range(2)]
        x_ready = sem("x_ready")
        qk_sb = sem("qk_sb")
        negm_rd = sem("negm_rd")
        exp_rd = sem("exp_rd")
        p_rd = sem("p_rd")
        var_rd = sem("var_rd")
        std_rd = sem("std_rd")
        chosen_rd = sem("chosen_rd")
        route_rd = sem("route_rd")
        split_hi = sem("split_hi")
        split_rs = sem("split_rs")
        split_rd = sem("split_rd")
        ssilu = sem("ssilu")
        pos_rd = sem("pos_rd")
        dve_link = sem("dve_link")
        out_done = sem("out_done")

        class Pass:

            def __init__(self, tag, per_layer):
                self.per_layer = per_layer
                self.sel_rd = sem(f"{tag}_sel_rd")
                self.g_full = sem(f"{tag}_g_full")
                self.g_sb = sem(f"{tag}_g_sb")
                self.selT_ps = sem(f"{tag}_selT_ps")
                self.selT_sb = sem(f"{tag}_selT_sb")
                self.h_full = sem(f"{tag}_h_full")
                self.silu_rd = sem(f"{tag}_silu_rd")
                self.h_rd = sem(f"{tag}_h_rd")
                self.hT_ps = sem(f"{tag}_hT_ps")
                self.hT_sb = sem(f"{tag}_hT_sb")
                self.y_full = sem(f"{tag}_y_full")
                self.hi_rd = sem(f"{tag}_hi_rd")
                self.res_rd = sem(f"{tag}_res_rd")
                self.mid_rd = sem(f"{tag}_mid_rd")
                self.lo_rd = sem(f"{tag}_lo_rd")
                self.comb = sem(f"{tag}_comb")
        main = Pass("main", PAIRS)
        more = Pass("more", PAIRS * (ROUNDS - 1))
        gu_in = [sem(f"gu_in{b}") for b in range(3)]
        dn_in = [sem(f"dn_in{b}") for b in range(2)]
        mgu_in = [sem(f"mgu_in{b}") for b in range(3)]
        mdn_in = [sem(f"mdn_in{b}") for b in range(2)]
        main.w_in = (gu_in, dn_in)
        more.w_in = (mgu_in, mdn_in)

        block = ctx.enter_context(nc.Block())

        def stand_alone(eng):
            eng.sem_inc(carried, 1)

        def x_at(l, i, t):
            return x_ready, 4 * l + 2 * i + t + 2

        def x_before(l):
            return x_ready, 4 * l + 1

        def full_at(l, name):
            b = BANK_OF[name]
            return full[b], l * PER_BANK[b] + ORDER[name] + 1

        def read_at(l, name):
            b = BANK_OF[name]
            return read[b], l * PER_BANK[b] + ORDER[name] + 2

        def free_at(l, name):
            b = BANK_OF[name]
            return read[b], l * PER_BANK[b] + ORDER[name] + 1

        def pairs_of_pass(eng, base, body, start=0):
            for q in range(start, PEELED):
                body(base + q, q, q % 3, q % 2, q // 3, q == 0, False)
            with eng.Fori(0, (PAIRS - PEELED) // PAIR_STEP - 1) as i:
                for j in range(PEELED, PEELED + PAIR_STEP):
                    body(base + PAIR_STEP * i + j, PAIR_STEP * i + j, j % 3, j % 2, PAIR_STEP // 3 * i + j // 3,
                         False, False)
            for q in range(PAIRS - PAIR_STEP, PAIRS):
                body(base + q, q, q % 3, q % 2, q // 3, False, q == PAIRS - 1)

        def passes(eng, l, run, skipped):
            run(main, l, None)
            eng.wait_ge(route_rd, l + 1)
            stand_alone(eng)
            cnt = eng.value_load(counts_i[0:1, 0:1], min_val=0, max_val=S)
            with eng.If(cnt > SLOTS):
                eng.wait_ge(main.comb, l * PAIRS + PAIRS)
                stand_alone(eng)
                with eng.Fori(0, ROUNDS - 1) as r:
                    run(more, l * (ROUNDS - 1) + r, l * (ROUNDS - 1) + r)
                eng.nop()
            with eng.Else():
                skipped(more.per_layer)
                eng.nop()

        @block.sync
        def _(sp):
            sp.dma_start(cst[:], consts).then_inc(const_in, 16)
            kvv = w_mem_kv.rearrange("l (p k) n -> l p k n", k=KD)
            win = w_in.rearrange("l (p k) n -> l p k n", k=KD)
            wov = w_out.rearrange("l (k p) n -> l p k n", p=P)
            sgv = ws_gate.rearrange("l (p k) n -> l p k n", k=KD)
            suv = ws_up.rearrange("l (p k) n -> l p k n", k=KD)
            sdv = ws_down.rearrange("l (p k) n -> l p k n", k=KF)
            gv = w_gate.rearrange("l (r e) (p k) n -> (l r) p e (k n)", e=2, k=KD)
            uv = w_up.rearrange("l (r e) (p k) n -> (l r) p e (k n)", e=2, k=KD)
            dv = w_down.rearrange("l (r e) (p k) n -> (l r) p e (k n)", e=2, k=KF)

            def chunk(l, c):
                half = c % 2
                if c >= 2:
                    sp.wait_ge(*full_at(l, LAST_USE[c - 2]))
                dst = stage[:, half, :].rearrange("p (k n) -> p k n", k=KD)
                name = CHUNKS[c]
                stand_alone(sp)
                s_in = chunk_in[half]
                if name == "sgu":
                    sp.dma_start(dst[:, :, 0:256], sgv[l]).then_inc(s_in, 16)
                    sp.dma_start(dst[:, :, 256:512], suv[l]).then_inc(s_in, 16)
                elif name == "mem":
                    for t in range(2):
                        sp.dma_start(mem_sb[:, t, :], mem[0, t * P:(t + 1) * P, :]).then_inc(s_in, 16)
                elif name == "uqm":
                    for j, at in ((0, 0), (1, POOL_W + 3 * 512)):
                        sp.dma_start(dst[:, :, j * 256:(j + 1) * 256], win[l][:, :, at:at + 256]).then_inc(s_in, 16)
                else:
                    if name == "kv":
                        src = kvv[l]
                    elif name in ("q", "k", "v"):
                        at = POOL_W + 512 * "qkv".index(name)
                        src = win[l][:, :, at:at + 512]
                    elif name in ("wo0", "wo1"):
                        at = 512 * int(name[2])
                        src = wov[l][:, :, at:at + 512]
                    else:
                        src, dst = sdv[l], stage[:, half, 0:KF * D].rearrange("p (k n) -> p k n", k=KF)
                    cut = src.shape[1] // 2
                    sp.dma_start(dst[:, 0:cut], src[:, 0:cut]).then_inc(s_in, 16)
                    sp.dma_start(dst[:, cut:], src[:, cut:]).then_inc(s_in, 16)

            def load_gu(ps, l, q, g, n_free, free=None):
                if n_free is not None:
                    sp.wait_ge(ps.h_full, n_free)
                for j, src in ((0, gv), (1, uv)):
                    if free is not None:
                        sp.wait_ge(*full_at(l, free[j]))
                        stand_alone(sp)
                    sp.dma_start(GU[g][:, :, j, :, :].rearrange("p e k n -> p e (k n)"), src[l * PAIRS + q])\
                        .then_inc(ps.w_in[0][g], 16)

            def load_dn(ps, l, q, b, n_free):
                if n_free is not None:
                    sp.wait_ge(ps.y_full, 2 * n_free)
                sp.dma_start(dn[:, b].rearrange("p e k n -> p e (k n)"), dv[l * PAIRS + q]).then_inc(ps.w_in[1][b], 16)

            with sp.Fori(0, DEPTH) as l:
                chunk(l, 0)
                chunk(l, 1)
                sp.wait_ge(*x_before(l))
                chunk(l, 2)
                chunk(l, 3)
                sp.dma_start(wr[:], w_router.rearrange("l (p k) e -> l p k e", k=KD)[l]).then_inc(small_in, 16)
                sp.dma_start(rb[:], router_bias.rearrange("l (o e) -> l o e", o=1)[l].to_broadcast([P, E])).then_inc(small_in, 16)
                for g2 in range(2):
                    sp.dma_start(wp[64 * g2:64 * g2 + 64], w_pool.rearrange("l (j h) c d -> l h c j d", h=2)[l, g2]).then_inc(small_in, 16)
                sp.dma_start(psc[:], pool_scale.rearrange("l (j p) -> l p j", p=P)[l], allow_slow_non_contiguous=True).then_inc(small_in, 16)
                sp.dma_start(r8[:], pool_mat).then_inc(pool_in, 16)
                for c in range(4, 6):
                    chunk(l, c)
                load_gu(main, l, 0, 0, None)
                load_dn(main, l, 0, 0, None)
                chunk(l, 6)
                chunk(l, 7)
                load_gu(main, l, 1, 1, None)
                load_dn(main, l, 1, 1, None)
                sp.wait_ge(*full_at(l, "pooled"))
                sp.dma_start(lng, ln1_g.rearrange("l (o d) -> l o d", o=1)[l].to_broadcast([P, D])).then_inc(ln_in, 16)
                sp.dma_start(lnb, ln1_b.rearrange("l (o d) -> l o d", o=1)[l].to_broadcast([P, D])).then_inc(ln_in, 16)
                chunk(l, 8)
                chunk(l, 9)
                sp.wait_ge(*x_at(l, 0, NT - 1))
                sp.dma_start(lng, ln2_g.rearrange("l (o d) -> l o d", o=1)[l].to_broadcast([P, D])).then_inc(ln_in, 16)
                sp.dma_start(lnb, ln2_b.rearrange("l (o d) -> l o d", o=1)[l].to_broadcast([P, D])).then_inc(ln_in, 16)

                def run(ps, turn, round_):
                    base = turn * PAIRS
                    if round_ is None:
                        load_gu(ps, l, 2, 2, None, free=("sh1", "acc3"))
                    else:
                        for q in range(2):
                            load_gu(ps, l, q, q, None)
                            load_dn(ps, l, q, q, None)
                        load_gu(ps, l, 2, 2, None)

                    def body(n, q, g, b, use, first, last):
                        if not last:
                            load_gu(ps, l, q + 1, (g + 1) % 3, n - 1)
                        load_dn(ps, l, q, b, n - 1)
                    pairs_of_pass(sp, base, body, start=PEELED)
                    if round_ is not None:
                        sp.wait_ge(ps.comb, base + PAIRS)
                        stand_alone(sp)

                def skipped(n):
                    for g in range(3):
                        sp.sem_inc(mgu_in[g], n // PAIRS * USES[g] * 32)
                    for b in range(2):
                        sp.sem_inc(mdn_in[b], n * 8)
                passes(sp, l, run, skipped)
            for t in range(NT):
                sp.wait_ge(*x_at(DEPTH - 1, 1, t))
                sp.dma_start(out[0, t * P:(t + 1) * P, :], xs[:, t, :]).then_inc(out_done, 16)
            sp.wait_ge(out_done, 16 * NT)

        @block.tensor
        def _(pe):
            pe.wait_ge(const_in, 16)
            pe.wait_ge(setup_done, 1)
            layer = [None]

            def fill(l, name):
                pe.wait_ge(*free_at(l, name))
                return bank[BANK_OF[name]]

            def filled(l, name, ins):
                ins.then_inc(full[BANK_OF[name]], 1)

            def chunk_wait(l, c):
                pe.wait_ge(chunk_in[c % 2], l * 16 * len(CHUNKS) + 32 * (c // 2 + 1))

            def transposes(l, tag, src, tile_ready):
                for t in range(NT):
                    for w in tile_ready(t):
                        pe.wait_ge(*w)
                    for g in range(4):
                        o = fill(l, f"{tag}{g}") if t == 0 else bank[BANK_OF[f"{tag}{g}"]]
                        for kk in range(2):
                            m = pe.transpose(o[:, kk * S + t * P:kk * S + t * P + P], src[:, t, 2 * g + kk::KD], ident)
                        if t == NT - 1:
                            filled(l, f"{tag}{g}", m)

            def gather(ps, n, half, g_free):
                for w in g_free:
                    pe.wait_ge(*w)
                for kk in range(4):
                    k = 4 * half + kk
                    for j in range(3 * NT):
                        t, s = j // 3, j % 3
                        m = pe.matmul(G[:, kk * P:(kk + 1) * P], xsp[:, t, s, k::KD], sel[:, t, :],
                                      start=j == 0, stop=j == 3 * NT - 1)
                m.then_inc(ps.g_full, 1)

            def turn_sel(ps, n, q):
                pe.wait_ge(ps.g_sb, 2 * n + 2)
                gb = G[:].bitcast(BF16)
                for t in range(NT):
                    pe.transpose(gb[:, t * P:(t + 1) * P], sel[:, t, :], identb[:])
                for t in range(NT):
                    wq = w3[:, t].rearrange("p (r e) s -> p r (e s)", e=2)
                    m = pe.matmul(G[:, 256:262], sel[:, t, :], wq[:, q, :],
                                  start=t == 0, stop=t == NT - 1)
                m.then_inc(ps.selT_ps, 1)

            def combine(ps, n, b):
                pe.wait_ge(ps.lo_rd, 2 * n + 2)
                for t in range(NT):
                    for half in range(2):
                        for s in range(3):
                            m = pe.matmul(acc[2 * t + half][:, :], selT[:, b, t * P:(t + 1) * P],
                                          ysp[:, s, half * 512:(half + 1) * 512],
                                          start=False, stop=False, skip_group_check=True)
                m.then_inc(ps.comb, 1)

            def shared_turn(l):
                o = fill(l, "shT")
                for t in range(NT):
                    pe.wait_ge(*read_at(l, f"sh{t}"))
                    for kc in range(KF):
                        m = pe.transpose(o[:, (2 * t + kc) * P:(2 * t + kc + 1) * P], hh[:, t, kc::KF], ident)
                filled(l, "shT", m)

            def shared_down(l):
                pe.wait_ge(*read_at(l, "shT"))
                chunk_wait(l, 9)
                wd = stage[:, 1, 0:KF * D].rearrange("p (k n) -> p k n", k=KF)
                for t in range(NT):
                    for half in range(2):
                        name = f"acc{2 * t + half}"
                        o = fill(l, name)
                        for kc in range(KF):
                            m = pe.matmul(o[:, :], hT[:, (2 * t + kc) * P:(2 * t + kc + 1) * P],
                                          wd[:, kc, half * 512:(half + 1) * 512],
                                          start=kc == 0, stop=kc == KF - 1, skip_group_check=True)
                        filled(l, name, m)

            def run(ps, turn, round_):
                base = turn * PAIRS
                if round_ is None:
                    pe.wait_ge(*read_at(layer[0], "sh0"))
                pe.wait_ge(ps.sel_rd, base + 1)
                gather(ps, base, 0, [])
                if round_ is None:
                    shared_turn(layer[0])
                gather(ps, base, 1, [(ps.g_sb, 2 * base + 1)])
                if round_ is None:
                    shared_down(layer[0])
                turn_sel(ps, base, 0)

                def body(n, q, g, b, use, first, last):
                    pe.wait_ge(ps.g_sb, 2 * n + 2)
                    pe.wait_ge(ps.w_in[0][g], (turn * USES[g] + use) * 32 + 32)
                    if not first:
                        pe.wait_ge(ps.hT_sb, n)
                    for k in range(KD):
                        for a in range(2):
                            m = pe.matmul(H[64 * a:64 * a + 64, :], xg[:, k, 64 * a:64 * a + 64],
                                          GU[g][:, a, :, k, :], start=k == 0, stop=k == KD - 1)
                    m.then_inc(ps.h_full, 1)
                    if not last:
                        pe.wait_ge(ps.sel_rd, n + 2)
                        gather(ps, n + 1, 0, [(ps.selT_sb, n + 1)])
                    if not first:
                        combine(ps, n - 1, 1 - b)
                    pe.wait_ge(ps.h_rd, n + 1)
                    for kc in range(KF):
                        m = pe.transpose(H[:, kc * P:(kc + 1) * P], hh[:, 0, kc::KF], ident)
                    m.then_inc(ps.hT_ps, 1)
                    if not last:
                        gather(ps, n + 1, 1, [(ps.g_sb, 2 * n + 3)])
                    pe.wait_ge(ps.w_in[1][b], (n - b) * 8 + 16)
                    pe.wait_ge(ps.hT_sb, n + 1)
                    for half in range(2):
                        if not first:
                            pe.wait_ge(ps.res_rd, 2 * n - 1 + half)
                        for kc in range(KF):
                            for a in range(2):
                                m = pe.matmul(Y[half][64 * a:64 * a + 64, :],
                                              hT[:, kc * P + 64 * a:kc * P + 64 * a + 64],
                                              dn[:, b, a, kc, half * 512:(half + 1) * 512],
                                              start=kc == 0, stop=kc == KF - 1)
                        m.then_inc(ps.y_full, 1)
                    if not last:
                        turn_sel(ps, n + 1, q + 1)
                pairs_of_pass(pe, base, body)
                combine(ps, base + PAIRS - 1, 1)

            def skipped(n):
                for s_, k in ((more.g_full, 2), (more.selT_ps, 1), (more.h_full, 1), (more.hT_ps, 1),
                              (more.y_full, 2), (more.comb, 1)):
                    pe.sem_inc(s_, n * k)

            with pe.Fori(0, DEPTH) as l:
                layer[0] = l
                def mem_here(t):
                    chunk_wait(l, 0)
                    return []
                transposes(l, "memT", mem_sb, mem_here)
                chunk_wait(l, 1)
                for g in range(4):
                    pe.wait_ge(*read_at(l, f"memT{g}"))
                W = [stage[:, h, :].rearrange("p (k n) -> p k n", k=KD) for h in range(2)]
                o = fill(l, "kmT")
                for j in range(2):
                    for k in range(KD):
                        m = pe.matmul(o[:, j * S:(j + 1) * S], W[1][:, k, j * P:(j + 1) * P], memT[:, k, :],
                                      start=k == 0, stop=k == KD - 1)
                filled(l, "kmT", m)
                o = fill(l, "vm")
                for t in range(2):
                    for k in range(KD):
                        m = pe.matmul(o[:, t * 256:(t + 1) * 256], memT[:, k, t * P:(t + 1) * P], W[1][:, k, 256:512],
                                      start=k == 0, stop=k == KD - 1)
                filled(l, "vm", m)
                pe.wait_ge(x_in, 16)
                transposes(l, "xTa", xs, lambda t: [x_before(l)] if t == 0 else [])
                for g in range(4):
                    pe.wait_ge(*read_at(l, f"xTa{g}"))

                def rotate(i):
                    o = fill(l, f"rot{i}")
                    pe.wait_ge(*read_at(l, f"raw{i}"))
                    filled(l, f"rot{i}", pe.matmul(o[:, :], cc("rot"), raw[:, i % 2, :], start=True, stop=True))

                for i in range(4):
                    c = 2 + i // 2
                    if i % 2 == 0:
                        chunk_wait(l, c)
                    o = fill(l, f"raw{i}")
                    for j in range(2):
                        for k in range(KD):
                            m = pe.matmul(o[:, j * S:(j + 1) * S], W[c % 2][:, k, (2 * (i % 2) + j) * P:(2 * (i % 2) + j + 1) * P],
                                          xT[:, k, :], start=k == 0, stop=k == KD - 1)
                    filled(l, f"raw{i}", m)
                    if i:
                        rotate(i - 1)
                chunk_wait(l, 4)
                for t in range(NT):
                    o = fill(l, f"v{t}")
                    for k in range(KD):
                        m = pe.matmul(o[:, :], xT[:, k, t * P:(t + 1) * P], W[0][:, k, :],
                                      start=k == 0, stop=k == KD - 1)
                    filled(l, f"v{t}", m)
                    if t == 0:
                        rotate(3)

                def pool_inputs(t):
                    if t == 0:
                        chunk_wait(l, 5)
                        fill(l, "u")
                    o = bank[BANK_OF["u"]]
                    for k in range(KD):
                        m = pe.matmul(o[:, t * 256:(t + 1) * 256], xT[:, k, t * P:(t + 1) * P], W[1][:, k, 0:256],
                                      start=k == 0, stop=k == KD - 1)
                    if t == NT - 1:
                        filled(l, "u", m)

                def memory_queries(j):
                    if j == 0:
                        fill(l, "qm")
                    o = bank[BANK_OF["qm"]]
                    for k in range(KD):
                        m = pe.matmul(o[:, j * S:(j + 1) * S], W[1][:, k, 256 + j * P:256 + (j + 1) * P], xT[:, k, :],
                                      start=k == 0, stop=k == KD - 1)
                    if j == 1:
                        filled(l, "qm", m)

                def pool_tokens():
                    pe.wait_ge(*read_at(l, "u"))
                    pe.wait_ge(pool_in, 16 * l + 16)
                    o = fill(l, "pooled")
                    for g in range(4):
                        h0 = 64 * (g % 2)
                        for t in range(NT):
                            m = pe.matmul(o[h0:h0 + 64, (g // 2) * S:(g // 2 + 1) * S], uu[:, t, 64 * g:64 * g + 64],
                                          pool_sb[:, t, g, :], start=t == 0, stop=t == NT - 1)
                    filled(l, "pooled", m)

                def pool_channels():
                    pe.wait_ge(*read_at(l, "pooled"))
                    pe.wait_ge(small_in, 80 * l + 80)
                    o = fill(l, "pmix")
                    stand_alone(pe)
                    for g in range(4):
                        h0 = 64 * (g % 2)
                        m = pe.matmul(o[h0:h0 + 64, (g // 2) * S:(g // 2 + 1) * S], wp[h0:h0 + 64, g // 2, :],
                                      pooledT[h0:h0 + 64, g // 2, :], start=True, stop=True)
                    filled(l, "pmix", m)

                def project(i, ks):
                    name, t, half = f"wo{i}", i // 2, i % 2
                    if ks[0] == 0:
                        chunk_wait(l, 6 + half)
                        fill(l, name)
                    o = bank[BANK_OF[name]]
                    for k in ks:
                        pe.wait_ge(*read_at(l, "pmix" if k < 2 else f"o{k - 2}"))
                        m = pe.matmul(o[:, :], mixT[:, k, t * P:(t + 1) * P], W[half][:, k, :],
                                      start=k == 0, stop=k == KD - 1, skip_group_check=True)
                    if ks[-1] == KD - 1:
                        filled(l, name, m)
                beside = {0: [(pool_inputs, 0)], 1: [(pool_inputs, 1)], 2: [(memory_queries, 0)],
                          3: [(memory_queries, 1)], 4: [(pool_tokens,)], 5: [(pool_channels,)],
                          6: [(project, 0, [0, 1, 2, 3])], 7: [(project, 1, [0, 1, 2, 3])],
                          8: [(project, 0, [4]), (project, 1, [4])],
                          9: [(project, 0, [5]), (project, 1, [5])]}
                pe.wait_ge(qk_sb, 4 * l + 4)
                for name in ("v0", "v1", "kmT", "vm"):
                    pe.wait_ge(*read_at(l, name))

                def scores(u):
                    h0, c = 64 * (u % 2), u // 2
                    if u == DSA_HEADS:
                        pe.wait_ge(*read_at(l, "qm"))
                    o = fill(l, f"s{u}")
                    if u < DSA_HEADS:
                        q, k = qkT[h0:h0 + 64, c, :], qkT[h0:h0 + 64, 4 + c, :]
                        pe.matmul(o[:, 0:P], q[:, 0:P], k[:, 0:P], start=True, stop=True)
                        m = pe.matmul(o[:, P:3 * P], q[:, P:S], k, start=True, stop=True)
                    else:
                        c -= 4
                        for t in range(NT):
                            m = pe.matmul(o[:, t * S:(t + 1) * S], qmT[h0:h0 + 64, c, t * P:(t + 1) * P],
                                          kmT[h0:h0 + 64, c, :], start=True, stop=True)
                    filled(l, f"s{u}", m)

                def turn_probs(u):
                    o = fill(l, f"pT{u}")
                    pe.wait_ge(p_rd, UNITS * l + u + 1)
                    src = (0, 1, 2) if u < DSA_HEADS else (0, 2, 1, 3)
                    for j, s_ in enumerate(src):
                        m = pe.transpose(o[:, j * P:(j + 1) * P], prob[:, u % 2, s_ * P:(s_ + 1) * P], ident)
                    filled(l, f"pT{u}", m)

                def outputs(u):
                    h0 = 64 * (u % 2)
                    o = bank[BANK_OF[f"o{u // 2}"]]
                    if u % 2 == 0:
                        fill(l, f"o{u // 2}")
                    pe.wait_ge(*read_at(l, f"pT{u}"))
                    pt = pT[:, u % 2, :]
                    if u < DSA_HEADS:
                        pe.matmul(o[h0:h0 + 64, 0:S], vv[:, 0, 64 * u:64 * u + 64], pt[:, 0:S], start=True, stop=False)
                        m = pe.matmul(o[h0:h0 + 64, P:S], vv[:, 1, 64 * u:64 * u + 64], pt[:, S:S + P], start=False, stop=True)
                    else:
                        h = u - DSA_HEADS
                        for t in range(2):
                            m = pe.matmul(o[h0:h0 + 64, 0:S], vm[:, t, 64 * h:64 * h + 64], pt[:, t * S:(t + 1) * S],
                                          start=t == 0, stop=t == 1)
                    if u % 2:
                        filled(l, f"o{u // 2}", m)
                scores(0)
                for u in range(UNITS + 1):
                    if u + 1 < UNITS:
                        scores(u + 1)
                    for what, *args in beside.get(u, []):
                        what(*args)
                    if u < UNITS:
                        turn_probs(u)
                    if u:
                        outputs(u - 1)
                project(0, [6, 7])
                project(1, [6, 7])
                project(2, list(range(KD)))

                def turn_tile(t):
                    pe.wait_ge(*x_at(l, 0, t))
                    for j in range(2):
                        name = f"xTb{2 * t + j}"
                        o = fill(l, name)
                        for kk in range(4):
                            m = pe.transpose(o[:, kk * P:(kk + 1) * P], xs[:, t, 4 * j + kk::KD], ident)
                        filled(l, name, m)

                def router(t):
                    for j in range(2):
                        pe.wait_ge(*read_at(l, f"xTb{2 * t + j}"))
                    o = fill(l, f"logit{t}")
                    for k in range(KD):
                        m = pe.matmul(o[:, 0:E], xT[:, k, t * P:(t + 1) * P], wr[:, k, :],
                                      start=k == 0, stop=k == KD - 1)
                    filled(l, f"logit{t}", m)

                def shared_up(t, ks):
                    if ks[0] == 0:
                        fill(l, f"sh{t}")
                    o = bank[BANK_OF[f"sh{t}"]]
                    for k in ks:
                        m = pe.matmul(o[:, :], xT[:, k, t * P:(t + 1) * P], W[0][:, k, :],
                                      start=k == 0, stop=k == KD - 1)
                    if ks[-1] == KD - 1:
                        filled(l, f"sh{t}", m)
                turn_tile(0)
                project(3, list(range(KD)))
                router(0)
                chunk_wait(l, 8)
                shared_up(0, [0, 1, 2])
                turn_tile(1)
                shared_up(0, [3, 4])
                router(1)
                shared_up(0, [5, 6, 7])
                shared_up(1, list(range(KD)))
                o = fill(l, "cum")
                pe.wait_ge(chosen_rd, 2 * l + 2)
                ch = [chosenb[:, t * E:(t + 1) * E] for t in range(NT)]
                pe.matmul(o[:, 0:E], beforeb[:], ch[0], start=True, stop=True)
                pe.matmul(o[:, E:2 * E], onesb[:], ch[0], start=True, stop=False)
                pe.matmul(o[:, E:2 * E], beforeb[:], ch[1], start=False, stop=True)
                pe.matmul(o[:, 2 * E:3 * E], onesb[:], ch[0], start=True, stop=False)
                filled(l, "cum", pe.matmul(o[:, 2 * E:3 * E], onesb[:], ch[1], start=False, stop=True))
                pe.wait_ge(split_rd, 2 * l + 2)
                pe.wait_ge(route_rd, l + 1)
                passes(pe, l, run, skipped)

        @block.scalar
        def _(act):
            act.wait_ge(chunk_in[0], 32)
            act.dma_start(xs[:], x[0].rearrange("(t p) d -> p t d", p=P)).then_inc(x_in, 16)
            act.wait_ge(setup_done, 1)
            def copy(out_, in_, **kw):
                return act.activation(out_, in_, ACT.Copy, **kw)

            def take(l, name):
                act.wait_ge(*full_at(l, name))
                return bank[BANK_OF[name]]

            def evac(l, name, dst):
                copy(dst, take(l, name)[:, :]).then_inc(read[BANK_OF[name]], 1)

            def run(ps, turn, round_):
                base = turn * PAIRS
                def g_half(n, half):
                    act.wait_ge(ps.g_full, 2 * n + half + 1)
                    copy(xg[:, 4 * half:4 * half + 4, :].rearrange("p k c -> p (k c)"), G[:, :]).then_inc(ps.g_sb, 1)
                g_half(base, 0)
                g_half(base, 1)

                def body(n, q, g, b, use, first, last):
                    act.wait_ge(ps.h_full, n + 1)
                    act.activation(sg[:, 0, :], H[:, 0:F], ACT.Silu).then_inc(ps.silu_rd, 1)
                    if not last:
                        g_half(n + 1, 0)
                        g_half(n + 1, 1)
                    act.wait_ge(ps.selT_sb, n + 1)
                    for half in range(2):
                        act.wait_ge(ps.y_full, 2 * n + half + 1)
                        copy(ysp[:, 0, half * 512:(half + 1) * 512], Y[half][:, :], scale=wslot[:, b:b + 1])\
                            .then_inc(ps.hi_rd, 1)
                    for half in range(2):
                        act.wait_ge(ps.res_rd, 2 * n + half + 1)
                        copy(ysp[:, 1, half * 512:(half + 1) * 512], yres[:, half * 512:(half + 1) * 512])\
                            .then_inc(ps.mid_rd, 1)
                pairs_of_pass(act, base, body)

            def skipped(n):
                for s_, k in ((more.g_sb, 2), (more.silu_rd, 1), (more.hi_rd, 2), (more.mid_rd, 2)):
                    act.sem_inc(s_, n * k)

            with act.Fori(0, DEPTH) as l:
                for g in range(4):
                    evac(l, f"memT{g}", memT[:, 2 * g:2 * g + 2, :].rearrange("p k s -> p (k s)"))
                evac(l, "kmT", kmT.rearrange("p k s -> p (k s)"))
                evac(l, "vm", vm.rearrange("p k s -> p (k s)"))
                for g in (0, 2):
                    evac(l, f"xTa{g}", xT[:, 2 * g:2 * g + 2, :].rearrange("p k s -> p (k s)"))
                for i in range(4):
                    if i >= 2:
                        act.wait_ge(qk_sb, 4 * l + i - 1)
                    evac(l, f"raw{i}", raw[:, i % 2, :])
                evac(l, "v0", vv[:, 0, :])
                evac(l, "v1", vv[:, 1, :])

                def exps(u):
                    act.wait_ge(negm_rd, UNITS * l + u + 1)
                    if u < DSA_HEADS:
                        for t, a, z in ((0, 0, P), (1, P, 3 * P)):
                            m = act.activation(prob[:, u % 2, a:z], prob[:, u % 2, a:z], ACT.Exp,
                                               bias=negm[u % 2][:, t:t + 1], scale=SCALE)
                        m.then_inc(exp_rd, 1)
                    else:
                        if u >= 2:
                            act.wait_ge(*full_at(l, f"pT{u - 2}"))
                        s_ = take(l, f"s{u}")
                        for t in range(NT):
                            m = act.activation(prob[:, u % 2, t * S:(t + 1) * S], s_[:, t * S:(t + 1) * S], ACT.Exp,
                                               bias=negm[u % 2][:, t:t + 1], scale=SCALE,
                                               accum_out=den[u % 2][:, t:t + 1])
                        m.then_inc(read[BANK_OF[f"s{u}"]], 1)

                def turned(u):
                    w = 3 * P if u < DSA_HEADS else 4 * P
                    if u >= 2:
                        act.wait_ge(*full_at(l, f"o{(u - 2) // 2}"))
                    s_ = take(l, f"pT{u}")
                    copy(pT[:, u % 2, 0:w], s_[:, 0:w]).then_inc(read[BANK_OF[f"pT{u}"]], 1)

                def heads_out(c):
                    name = f"o{c}"
                    copy(mixT[:, 2 + c, :], take(l, name)[:, 0:S]).then_inc(read[BANK_OF[name]], 1)
                for u in range(UNITS):
                    exps(u)
                    if u >= 3 and u % 2:
                        heads_out((u - 3) // 2)
                    if u:
                        turned(u - 1)
                    if u == 2:
                        evac(l, "u", uu.rearrange("p t n -> p (t n)"))
                    if u == 4:
                        evac(l, "qm", qmT.rearrange("p k s -> p (k s)"))
                turned(UNITS - 1)
                heads_out(UNITS // 2 - 1)

                def sqrt(i, t):
                    act.wait_ge(var_rd, 4 * l + 2 * i + t + 1)
                    act.activation(std[:, t:t + 1], mv[:, t, 1:2], ACT.Sqrt, bias=epst[:, 0:1]).then_inc(std_rd, 1)

                def split(t, part):
                    if part == 0:
                        act.wait_ge(*x_at(l, 0, t))
                        copy(xsp[:, t, 0, :], xs[:, t, :]).then_inc(split_hi, 1)
                    else:
                        act.wait_ge(split_rs, 2 * l + t + 1)
                        copy(xsp[:, t, 1, :], xres[:, t, :]).then_inc(split_hi, 1)
                def turned_tile(t):
                    for j in range(2):
                        name = f"xTb{2 * t + j}"
                        copy(xT[:, 4 * j:4 * j + 4, t * P:(t + 1) * P],
                             take(l, name)[:, :].rearrange("p (k s) -> p k s", k=4)).then_inc(read[BANK_OF[name]], 1)

                def exp_logits(t):
                    name = f"logit{t}"
                    act.activation(sig[:, t * E:(t + 1) * E], take(l, name)[:, 0:E], ACT.Exp, scale=-1.0)\
                        .then_inc(read[BANK_OF[name]], 1)
                sqrt(0, 0)
                split(0, 0)
                turned_tile(0)
                sqrt(0, 1)
                exp_logits(0)
                turned_tile(1)
                split(1, 0)
                exp_logits(1)
                split(0, 1)
                split(1, 1)
                for t in range(NT):
                    act.wait_ge(*full_at(l, f"sh{t}"))
                    act.activation(sg[:, t, :], bank[BANK_OF[f"sh{t}"]][:, 0:F], ACT.Silu).then_inc(ssilu, 1)
                passes(act, l, run, skipped)
                for t in range(NT):
                    sqrt(1, t)

        @block.vector
        def _(dve):
            dve.memset(onesb[:], 1.0)
            dve.memset(epst[:], EPS)
            dve.memset(small[:], 0.0)
            dve.wait_ge(const_in, 16)
            dve.tensor_copy(identb[:], ident)
            dve.tensor_copy(beforeb[:], cc("before")).then_inc(setup_done, 1)
            for s_ in [*read, x_ready]:
                dve.sem_inc(s_, 1)
            links = [0]
            layer = [None]

            def link(ins):
                links[0] += 1
                ins.then_inc(dve_link, 1)
                dve.wait_ge(dve_link, layer[0] * DVE_LINKS + links[0])

            def take(l, name):
                dve.wait_ge(*full_at(l, name))
                return bank[BANK_OF[name]]

            def evac(l, name, dst):
                dve.tensor_copy(dst, take(l, name)[:, :]).then_inc(read[BANK_OF[name]], 1)

            def residual_stats(l, i, t, names):
                for h in range(2):
                    v = xs[:, t, h * 512:(h + 1) * 512]
                    dve.scalar_tensor_tensor(v, v, ALPHA, take(l, names[h])[:, :], ALU.mult, ALU.add)\
                        .then_inc(read[BANK_OF[names[h]]], 1)
                for h in range(2):
                    dve.wait_ge(*read_at(l, names[h]))
                    m = dve.bn_stats(stats[:, t, h, :], xs[:, t, h * 512:(h + 1) * 512])
                link(m)
                stand_alone(dve)
                dve.bn_aggr(mv[:, t, :], stats[:, t, :, :]).then_inc(var_rd, 1)

            def normalised(l, i, t):
                dve.wait_ge(std_rd, 4 * l + 2 * i + t + 1)
                dve.reciprocal(rstd[:, t:t + 1], std[:, t:t + 1])
                dve.wait_ge(ln_in, 64 * l + 32 * i + 32)
                v = xs[:, t, :]
                link(dve.scalar_tensor_tensor(v, v, mv[:, t, 0:1], lng, ALU.subtract, ALU.mult))
                dve.scalar_tensor_tensor(v, v, rstd[:, t:t + 1], lnb, ALU.mult, ALU.add).then_inc(x_ready, 1)

            def split_residual(l, t):
                dve.wait_ge(split_hi, 4 * l + t + 1)
                dve.tensor_tensor(xres[:, t, :], xs[:, t, :], xsp[:, t, 0, :], ALU.subtract).then_inc(split_rs, 1)

            def split_last(l, t):
                dve.wait_ge(split_hi, 4 * l + 2 + t + 1)
                dve.tensor_tensor(xsp[:, t, 2, :], xres[:, t, :], xsp[:, t, 1, :], ALU.subtract).then_inc(split_rd, 1)

            def run(ps, turn, round_):
                base = turn * PAIRS
                if round_ is not None:
                    dve.tensor_scalar(pos, pos, -float(SLOTS), None, ALU.add).then_inc(pos_rd, 1)
                    dve.wait_ge(pos_rd, round_ + 1)
                slots = cc("slot").unsqueeze(1).to_broadcast([P, 2, SLOTS])
                posv = pos.rearrange("p (t r e) -> p t r e", t=NT, e=2)

                def build_sel(n, q, wait):
                    if wait:
                        dve.wait_ge(ps.selT_ps, n)
                    for t in range(NT):
                        m = dve.tensor_tensor(sel[:, t, :].rearrange("p (e c) -> p e c", e=2), slots,
                                              posv[:, t, q, :].unsqueeze(2).to_broadcast([P, 2, SLOTS]), ALU.is_equal)
                    m.then_inc(ps.sel_rd, 1)

                def take_selT(n, b):
                    dve.wait_ge(ps.selT_ps, n + 1)
                    dve.tensor_copy(selT[:, b, :], G[:].bitcast(BF16)[:, 0:S])
                    for e in range(2):
                        m = dve.tensor_reduce(wslot[64 * e:64 * e + 64, b:b + 1], G[64 * e:64 * e + 64, 256 + 3 * e:259 + 3 * e],
                                              AX.X, ALU.add)
                    m.then_inc(ps.selT_sb, 1)
                build_sel(base, 0, False)
                if round_ is None:
                    l = layer[0]
                    for t in range(NT):
                        dve.wait_ge(ssilu, 2 * l + t + 1)
                        name = f"sh{t}"
                        dve.tensor_tensor(hh[:, t, :], sg[:, t, :], take(l, name)[:, F:2 * F], ALU.mult)\
                            .then_inc(read[BANK_OF[name]], 1)
                    evac(l, "shT", hT)
                take_selT(base, 0)

                def body(n, q, g, b, use, first, last):
                    if not last:
                        build_sel(n + 1, q + 1, True)
                    dve.wait_ge(ps.silu_rd, n + 1)
                    dve.tensor_tensor(hh[:, 0, :], sg[:, 0, :], H[:, F:2 * F], ALU.mult).then_inc(ps.h_rd, 1)
                    dve.wait_ge(ps.hT_ps, n + 1)
                    dve.tensor_copy(hT[:, 0:F], H[:, 0:F]).then_inc(ps.hT_sb, 1)
                    dve.wait_ge(ps.selT_sb, n + 1)
                    if not first:
                        dve.wait_ge(ps.lo_rd, 2 * n)
                    for half in range(2):
                        dve.wait_ge(ps.hi_rd, 2 * n + half + 1)
                        dve.scalar_tensor_tensor(yres[:, half * 512:(half + 1) * 512], Y[half][:, :], wslot[:, b:b + 1],
                                                 ysp[:, 0, half * 512:(half + 1) * 512], ALU.mult, ALU.subtract)\
                            .then_inc(ps.res_rd, 1)
                    if not last:
                        take_selT(n + 1, 1 - b)
                    for half in range(2):
                        dve.wait_ge(ps.mid_rd, 2 * n + half + 1)
                        dve.tensor_tensor(ysp[:, 2, half * 512:(half + 1) * 512], yres[:, half * 512:(half + 1) * 512],
                                          ysp[:, 1, half * 512:(half + 1) * 512], ALU.subtract).then_inc(ps.lo_rd, 1)
                pairs_of_pass(dve, base, body)
                dve.wait_ge(ps.comb, base + PAIRS)

            def skipped(n):
                for s_, k in ((more.sel_rd, 1), (more.selT_sb, 1), (more.h_rd, 1), (more.hT_sb, 1),
                              (more.res_rd, 2), (more.lo_rd, 2)):
                    dve.sem_inc(s_, n * k)
                dve.sem_inc(pos_rd, n // PAIRS)

            with dve.Fori(0, DEPTH) as l:
                layer[0] = l
                links[0] = 0
                for g in (1, 3):
                    evac(l, f"xTa{g}", xT[:, 2 * g:2 * g + 2, :].rearrange("p k s -> p (k s)"))
                cos2 = cc("cos").unsqueeze(1).to_broadcast([P, 2, S])
                sin2 = cc("sin").unsqueeze(1).to_broadcast([P, 2, S])
                for i in range(4):
                    dve.wait_ge(*read_at(l, f"raw{i}"))
                    dst = qkT[:, 2 * i:2 * i + 2, :]
                    dve.tensor_tensor(dst, raw[:, i % 2, :].rearrange("p (c s) -> p c s", s=S), cos2, ALU.mult)
                    r_ = take(l, f"rot{i}")
                    if i:
                        dve.wait_ge(qk_sb, 4 * l + i)
                    m = dve.tensor_tensor(rt.rearrange("p (c s) -> p c s", s=S), r_[:, :].rearrange("p (c s) -> p c s", s=S),
                                          sin2, ALU.mult)
                    m.then_inc(read[BANK_OF[f"rot{i}"]], 1)
                    dve.wait_ge(*read_at(l, f"rot{i}"))
                    dve.tensor_tensor(dst, dst, rt.rearrange("p (c s) -> p c s", s=S), ALU.add).then_inc(qk_sb, 1)

                def pool_scaled():
                    dve.wait_ge(small_in, 80 * l + 80)
                    o = take(l, "pmix")
                    for j in range(2):
                        m = dve.tensor_scalar(mixT[:, j, :], o[:, j * S:(j + 1) * S], psc[:, j:j + 1], None, ALU.mult)
                    m.then_inc(read[BANK_OF["pmix"]], 1)

                def maxima(u):
                    i = u % 2
                    o = take(l, f"s{u}")
                    if u < DSA_HEADS:
                        if u >= 2:
                            dve.wait_ge(*full_at(l, f"pT{u - 2}"))
                        stand_alone(dve)
                        for t, a, z in ((0, 0, P), (1, P, 3 * P)):
                            m = dve.tensor_tensor_reduce(prob[:, i, a:z], o[:, a:z], cc("bias")[:, a:z], 1.0, -3e38,
                                                         ALU.add, ALU.max, mx[i][:, t:t + 1])
                        m.then_inc(read[BANK_OF[f"s{u}"]], 1)
                        dve.wait_ge(*read_at(l, f"s{u}"))
                    else:
                        link(dve.tensor_reduce(mx[i], o[:, :].rearrange("p (t s) -> p t s", t=NT), AX.X, ALU.max))
                    dve.tensor_scalar(negm[i], mx[i], -SCALE, None, ALU.mult).then_inc(negm_rd, 1)

                def normalise(u):
                    i = u % 2
                    if u < DSA_HEADS:
                        dve.wait_ge(exp_rd, DSA_HEADS * l + u + 1)
                    else:
                        dve.wait_ge(*read_at(l, f"s{u}"))
                    cuts = ((0, 0, P), (1, P, 3 * P)) if u < DSA_HEADS else ((0, 0, S), (1, S, 2 * S))
                    if u < DSA_HEADS:
                        for t, a, z in cuts:
                            m = dve.tensor_tensor_reduce(prob[:, i, a:z], prob[:, i, a:z], cc("mult")[:, a:z], 1.0, 0.0,
                                                         ALU.mult, ALU.add, den[i][:, t:t + 1])
                        link(m)
                    link(dve.reciprocal(rden[i], den[i]))
                    for t, a, z in cuts:
                        m = dve.tensor_scalar(prob[:, i, a:z], prob[:, i, a:z], rden[i][:, t:t + 1], None, ALU.mult)
                    m.then_inc(p_rd, 1)

                maxima(0)
                for u in range(UNITS):
                    if u + 1 < UNITS:
                        maxima(u + 1)
                    normalise(u)
                    if u == 4:
                        evac(l, "pooled", pooledT.rearrange("p k s -> p (k s)"))
                    if u == 5:
                        pool_scaled()
                residual_stats(l, 0, 0, ("wo0", "wo1"))
                normalised(l, 0, 0)
                split_residual(l, 0)
                residual_stats(l, 0, 1, ("wo2", "wo3"))
                normalised(l, 0, 1)


                def route(t):
                    def tile(v, n=E):
                        return v[:, t * n:(t + 1) * n]
                    sig_, biased_, masked_, chosen_, wts_, wres_ = map(tile, (sig, biased, masked, chosen, wts, wres))
                    g8_, gs_, rank_, gneg_ = tile(g8, GROUPS * 8), tile(gs, GROUPS), tile(rank, GROUPS), tile(gneg, GROUPS)
                    dve.wait_ge(*read_at(l, f"logit{t}"))
                    link(dve.tensor_scalar(sig_, sig_, 1.0, None, ALU.add))
                    link(dve.reciprocal(sig_, sig_))
                    link(dve.tensor_tensor(biased_, sig_, rb[:], ALU.add))
                    stand_alone(dve)
                    for j in range(GROUPS):
                        m = dve.max(g8_[:, 8 * j:8 * j + 8], biased_[:, 8 * j:8 * j + 8])
                    link(m)
                    g8v = g8_.rearrange("p (j k) -> p j k", k=8)
                    link(dve.tensor_tensor(gs_, g8v[:, :, 0], g8v[:, :, 1], ALU.add))
                    other = gs_.unsqueeze(1).to_broadcast([P, GROUPS, GROUPS])
                    own = gs_.unsqueeze(2).to_broadcast([P, GROUPS, GROUPS])
                    c1 = cmp1.rearrange("p (i j) -> p i j", j=GROUPS)
                    c2 = cmp2.rearrange("p (i j) -> p i j", j=GROUPS)
                    dve.tensor_tensor(c1, other, own, ALU.is_gt)
                    link(dve.tensor_tensor(c2, other, own, ALU.is_equal))
                    link(dve.tensor_tensor(cmp2, cmp2, cc("tri"), ALU.mult))
                    link(dve.tensor_tensor(cmp1, cmp1, cmp2, ALU.add))
                    link(dve.tensor_reduce(rank_, c1, AX.X, ALU.add))
                    link(dve.tensor_scalar(rank_, rank_, float(TOP_GROUPS), None, ALU.is_lt))
                    link(dve.tensor_scalar(gneg_, rank_, BIG, -BIG, ALU.mult, ALU.add))
                    b3 = biased_.rearrange("p (j k) -> p j k", k=8)
                    m3 = masked_.rearrange("p (j k) -> p j k", k=8)
                    link(dve.tensor_tensor(m3, b3, rank_.unsqueeze(2).to_broadcast([P, GROUPS, 8]), ALU.mult))
                    link(dve.tensor_tensor(m3, m3, gneg_.unsqueeze(2).to_broadcast([P, GROUPS, 8]), ALU.add))
                    stand_alone(dve)
                    link(dve.max(tile(top, 8), masked_))
                    stand_alone(dve)
                    link(dve.match_replace(chosen_, tile(top, 8), masked_, GONE))
                    link(dve.tensor_scalar(chosen_, chosen_, GONE / 2, None, ALU.is_lt))
                    dve.tensor_copy(tile(chosenb), chosen_).then_inc(chosen_rd, 1)
                    link(dve.tensor_tensor_reduce(wts_, chosen_, sig_, 1.0, 0.0, ALU.mult, ALU.add, wsum[:, t:t + 1]))
                    link(dve.reciprocal(wrec[:, t:t + 1], wsum[:, t:t + 1]))
                    link(dve.tensor_scalar(wts_, wts_, wrec[:, t:t + 1], ROUTED_SCALE, ALU.mult, ALU.mult))
                    part3 = [w3[:, t, :, s_] for s_ in range(3)]
                    link(dve.tensor_copy(part3[0], wts_))
                    link(dve.tensor_tensor(wres_, wts_, part3[0], ALU.subtract))
                    link(dve.tensor_copy(part3[1], wres_))
                    dve.tensor_tensor(part3[2], wres_, part3[1], ALU.subtract)
                route(0)
                split_residual(l, 1)
                split_last(l, 0)
                route(1)
                o = take(l, "cum")
                link(dve.scalar_tensor_tensor(pos, o[:, 0:NT * E], 1.0, chosen, ALU.add, ALU.mult))
                dve.tensor_scalar(pos, pos, -1.0, None, ALU.add)
                m = dve.tensor_reduce(cntf, o[:, NT * E:(NT + 1) * E], AX.X, ALU.max)
                m.then_inc(read[BANK_OF["cum"]], 1)
                dve.wait_ge(*read_at(l, "cum"))
                dve.tensor_copy(counts_i[:], cntf).then_inc(route_rd, 1)
                split_last(l, 1)
                passes(dve, l, run, skipped)
                for t in range(NT):
                    residual_stats(l, 1, t, (f"acc{2 * t}", f"acc{2 * t + 1}"))
                for t in range(NT):
                    normalised(l, 1, t)
                assert links[0] == DVE_LINKS, links[0]


_INS = ["x", "mem", "w_in", "w_pool", "pool_scale", "w_mem_kv", "w_out", "ln1_g", "ln1_b", "w_router",
        "router_bias", "w_gate", "w_up", "w_down", "ws_gate", "ws_up", "ws_down", "ln2_g", "ln2_b"]


def kernel(**inputs):
    import concourse.bacc as bacc
    from concourse.bass_utils import run_bass_kernel_spmd

    nc = bacc.Bacc("TRN2", target_bir_lowering=False, num_devices=1)
    consts, pool_mat = constants()
    given = {n: np.ascontiguousarray(inputs[n]) for n in _INS}
    given["consts"], given["pool_mat"] = consts, pool_mat
    arrays, args = {}, []
    for name, a in given.items():
        arrays[f"in_{name}"] = a
        args.append(nc.dram_tensor(f"in_{name}", a.shape, mybir.dt.from_np(a.dtype), kind="ExternalInput").ap())
    args.append(nc.dram_tensor("out_x", (1, S, D), F32, kind="ExternalOutput").ap())
    build(nc, *args)
    r = run_bass_kernel_spmd(nc, [arrays], core_ids=[0])
    return r.results[0]["out_x"]
```
